# Optimizing a Trainium2 kernel written in Bass

```python
import jax, jax.numpy as jnp
from jax import lax
import numpy as np

D_MODEL = 1024
BATCH = 1
SEQ = 256
DEPTH = 1

D_MIX = D_MODEL
D_CONV = D_MIX // 2
D_ATTN = D_MIX - D_CONV
CONV_WIDTH = 3
ATTN_HEADS = 8
HEAD_DIM = D_ATTN // ATTN_HEADS
MOBA_BLOCK = 256
MOBA_TOPK = 3
Q_CHUNK = 128
D_PROJ = 3 * D_CONV + 3 * D_ATTN
PEER_HEADS = 8
PEER_NKEYS = 128
PEER_N = PEER_NKEYS * PEER_NKEYS
PEER_DKEY = 256
PEER_TOPK = 16
PEER_CHUNK = 128
EPS = 1e-6
NEG = -1e30

kernel_name = "hymba_conv_moba_peer_block"

def rmsnorm(x, g):
    xf = x.astype(jnp.float32)
    y = xf * lax.rsqrt(jnp.mean(xf * xf, axis=-1, keepdims=True) + EPS)
    return (y * g.astype(jnp.float32)).astype(x.dtype)

def short_conv_mixer(b_gate, c_gate, h, conv_w):
    u = c_gate * h
    y = lax.conv_general_dilated(
        u, conv_w[:, None, :].astype(u.dtype), window_strides=(1,),
        padding=[(CONV_WIDTH - 1, 0)], dimension_numbers=("NWC", "WIO", "NWC"),
        feature_group_count=D_CONV)
    return b_gate * y

def moba_attention(q, k, v):
    b_, s_, h_, hd = q.shape
    nb = -(-s_ // MOBA_BLOCK)
    pad = nb * MOBA_BLOCK - s_
    kp = jnp.pad(k, ((0, 0), (0, pad), (0, 0), (0, 0)))
    vp = jnp.pad(v, ((0, 0), (0, pad), (0, 0), (0, 0)))
    kb = kp.reshape(b_, nb, MOBA_BLOCK, h_, hd).transpose(0, 3, 1, 2, 4)
    vb = vp.reshape(b_, nb, MOBA_BLOCK, h_, hd).transpose(0, 3, 1, 2, 4)
    k_mean = jnp.mean(kb.astype(jnp.float32), axis=3)
    qh = q.transpose(0, 2, 1, 3)
    gate = jnp.einsum("bhsd,bhnd->bhsn", qh.astype(jnp.float32), k_mean)
    own = jnp.arange(s_, dtype=jnp.int32) // MOBA_BLOCK
    past = jnp.arange(nb, dtype=jnp.int32)[None, :] < own[:, None]
    gate = jnp.where(past[None, None], gate, NEG)
    k_sel = min(MOBA_TOPK, nb)
    _, sel = lax.top_k(gate, k_sel)
    valid = sel < own[None, None, :, None]

    nc = s_ // Q_CHUNK
    q_c = qh.reshape(b_, h_, nc, Q_CHUNK, hd).transpose(0, 2, 1, 3, 4).reshape(b_ * nc, h_, Q_CHUNK, hd)
    sel_c = sel.reshape(b_, h_, nc, Q_CHUNK, k_sel).transpose(0, 2, 1, 3, 4).reshape(b_ * nc, h_, Q_CHUNK, k_sel)
    val_c = valid.reshape(b_, h_, nc, Q_CHUNK, k_sel).transpose(0, 2, 1, 3, 4).reshape(b_ * nc, h_, Q_CHUNK, k_sel)
    b_idx = jnp.repeat(jnp.arange(b_, dtype=jnp.int32), nc)
    c_idx = jnp.tile(jnp.arange(nc, dtype=jnp.int32), b_)
    scale = 1.0 / math_sqrt(hd)

    def step(args):
        qc, selc, validc, bi, ci = args
        kbb = kb[bi]
        vbb = vb[bi]
        k_g = jax.vmap(lambda kh, sh: kh[sh])(kbb, selc)
        v_g = jax.vmap(lambda vh, sh: vh[sh])(vbb, selc)
        q_pos = ci * Q_CHUNK + jnp.arange(Q_CHUNK, dtype=jnp.int32)
        own_b = (ci * Q_CHUNK) // MOBA_BLOCK
        k_own = lax.dynamic_index_in_dim(kbb, own_b, axis=1, keepdims=False)
        v_own = lax.dynamic_index_in_dim(vbb, own_b, axis=1, keepdims=False)
        s_sel = jnp.einsum("hqd,hqkjd->hqkj", qc, k_g).astype(jnp.float32) * scale
        s_sel = jnp.where(validc[..., None], s_sel, NEG).reshape(h_, Q_CHUNK, k_sel * MOBA_BLOCK)
        s_own = jnp.einsum("hqd,hjd->hqj", qc, k_own).astype(jnp.float32) * scale
        k_pos = own_b * MOBA_BLOCK + jnp.arange(MOBA_BLOCK, dtype=jnp.int32)
        s_own = jnp.where(k_pos[None, None, :] <= q_pos[None, :, None], s_own, NEG)
        p = jax.nn.softmax(jnp.concatenate([s_sel, s_own], axis=-1), axis=-1)
        p_sel = p[..., : k_sel * MOBA_BLOCK].reshape(h_, Q_CHUNK, k_sel, MOBA_BLOCK).astype(v.dtype)
        p_own = p[..., k_sel * MOBA_BLOCK:].astype(v.dtype)
        return (jnp.einsum("hqkj,hqkjd->hqd", p_sel, v_g)
                + jnp.einsum("hqj,hjd->hqd", p_own, v_own))

    o = lax.map(step, (q_c, sel_c, val_c, b_idx, c_idx))
    o = o.reshape(b_, nc, h_, Q_CHUNK, hd).transpose(0, 1, 3, 2, 4)
    return o.reshape(b_, s_, h_ * hd)

def math_sqrt(n):
    return float(np.sqrt(n))

def peer_ffn(x, w_query, sub_keys1, sub_keys2, expert_down, expert_up):
    b_, s_, d_ = x.shape
    t = b_ * s_
    half = PEER_DKEY // 2

    def step(xc):
        qry = (xc @ w_query).reshape(PEER_CHUNK, PEER_HEADS, PEER_DKEY)
        s1 = jnp.einsum("chd,hnd->chn", qry[..., :half], sub_keys1).astype(jnp.float32)
        s2 = jnp.einsum("chd,hnd->chn", qry[..., half:], sub_keys2).astype(jnp.float32)
        v1, i1 = lax.top_k(s1, PEER_TOPK)
        v2, i2 = lax.top_k(s2, PEER_TOPK)
        cand = (v1[..., :, None] + v2[..., None, :]).reshape(PEER_CHUNK, PEER_HEADS, PEER_TOPK * PEER_TOPK)
        cidx = (i1[..., :, None] * PEER_NKEYS + i2[..., None, :]).reshape(PEER_CHUNK, PEER_HEADS, PEER_TOPK * PEER_TOPK)
        top_s, pos = lax.top_k(cand, PEER_TOPK)
        eidx = jnp.take_along_axis(cidx, pos, axis=-1)
        g = jax.nn.softmax(top_s, axis=-1).astype(xc.dtype)
        u = expert_down[eidx]
        act = jax.nn.gelu(jnp.einsum("chkd,cd->chk", u, xc), approximate=False)
        vv = expert_up[eidx]
        return jnp.einsum("chk,chkd->cd", g * act, vv)

    out = lax.map(step, x.reshape(t // PEER_CHUNK, PEER_CHUNK, d_))
    return out.reshape(b_, s_, d_)

def setup_inputs(seed: int = 0) -> dict:
    key = jax.random.key(seed)
    ks = jax.random.split(key, 16)
    f32 = jnp.float32
    nrm = lambda k, shape, sc: jax.random.normal(k, shape, f32) * sc
    gain = lambda k, n: 1.0 + 0.02 * jax.random.normal(k, (DEPTH, n), f32)
    return {
        "x": jax.random.normal(ks[0], (BATCH, SEQ, D_MODEL), f32),
        "norm_mix_g": gain(ks[1], D_MODEL),
        "w_in": nrm(ks[2], (DEPTH, D_MODEL, D_PROJ), D_MODEL ** -0.5),
        "conv_w": nrm(ks[3], (DEPTH, CONV_WIDTH, D_CONV), CONV_WIDTH ** -0.5),
        "norm_conv_out_g": gain(ks[4], D_CONV),
        "norm_attn_out_g": gain(ks[5], D_ATTN),
        "w_out": nrm(ks[6], (DEPTH, D_MIX, D_MODEL), D_MIX ** -0.5),
        "norm_ffn_g": gain(ks[7], D_MODEL),
        "peer_w_query": nrm(ks[8], (DEPTH, D_MODEL, PEER_HEADS * PEER_DKEY), D_MODEL ** -0.5),
        "peer_sub_keys1": nrm(ks[9], (DEPTH, PEER_HEADS, PEER_NKEYS, PEER_DKEY // 2), (PEER_DKEY // 2) ** -0.5),
        "peer_sub_keys2": nrm(ks[10], (DEPTH, PEER_HEADS, PEER_NKEYS, PEER_DKEY // 2), (PEER_DKEY // 2) ** -0.5),
        "peer_down": nrm(ks[11], (DEPTH, PEER_N, D_MODEL), D_MODEL ** -0.5),
        "peer_up": nrm(ks[12], (DEPTH, PEER_N, D_MODEL), 0.5),
        "final_norm_g": 1.0 + 0.02 * jax.random.normal(ks[13], (D_MODEL,), f32),
    }

def reference(x, norm_mix_g, w_in, conv_w, norm_conv_out_g, norm_attn_out_g, w_out,
              norm_ffn_g, peer_w_query, peer_sub_keys1, peer_sub_keys2, peer_down,
              peer_up, final_norm_g):
    b_, s_, _ = x.shape
    for l in range(DEPTH):
        h = rmsnorm(x, norm_mix_g[l])
        proj = h @ w_in[l]
        b_gate, c_gate, h_c, q, k, v = jnp.split(
            proj, [D_CONV, 2 * D_CONV, 3 * D_CONV, 3 * D_CONV + D_ATTN, 3 * D_CONV + 2 * D_ATTN], axis=-1)
        y_conv = short_conv_mixer(b_gate, c_gate, h_c, conv_w[l])
        y_attn = moba_attention(q.reshape(b_, s_, ATTN_HEADS, HEAD_DIM),
                                k.reshape(b_, s_, ATTN_HEADS, HEAD_DIM),
                                v.reshape(b_, s_, ATTN_HEADS, HEAD_DIM))
        mixed = jnp.concatenate([rmsnorm(y_conv, norm_conv_out_g[l]),
                                 rmsnorm(y_attn, norm_attn_out_g[l])], axis=-1)
        x = x + mixed @ w_out[l]
        x = x + peer_ffn(rmsnorm(x, norm_ffn_g[l]), peer_w_query[l], peer_sub_keys1[l],
                         peer_sub_keys2[l], peer_down[l], peer_up[l])
    return rmsnorm(x, final_norm_g)


_drawn_inputs = setup_inputs


def setup_inputs(seed=0):
    import zlib

    import numpy as np

    out = dict(_drawn_inputs(seed))
    spreads = {}
    factors = {}
    for name, (base, spread) in spreads.items():
        noise = np.random.default_rng([zlib.crc32(name.encode()), seed]).standard_normal(out[name].shape)
        drawn = base * np.exp(spread * noise) if base else spread * noise
        out[name] = __import__('jax').numpy.asarray(drawn.astype(out[name].dtype))
    for name, factor in factors.items():
        out[name] = (out[name] * factor).astype(out[name].dtype)
    return out
```

```python
import concourse.bass as bass
from concourse import mybir
from contextlib import ExitStack

P = 128
T = 256
TT = T // P
D = 1024
KC = D // P
HEADS, HD = 8, 64
NKEYS = 128
PH, TOPK = 8, 16
EPS = 1e-6
NEG = -1e30
LOWEST = -3.4e38

QK0, V0, CONV0, WOUT0, WQ0, DOWN0 = 0, 8, 12, 24, 32, 48
EARLY = 40
PAIR0 = DOWN0 + EARLY
PAIRS = NKEYS - EARLY
UP0 = PAIR0 + 2 * PAIRS
BLOCKS = UP0 + EARLY
RING = 4
MIXED_LO = UP0 + RING
QUAD = 4
GROUPS = T // QUAD

(ACT_SUMSQ1, ACT_ROOT1, ACT_X_HI, ACT_V, ACT_ROOT2, ACT_MIXED_HI, ACT_SUMSQ3, ACT_ROOT3, ACT_X2_HI, ACT_EXP,
 ACT_PICKED, ACT_SUMSQ4, ACT_SUMSQ4_B, ACT_ROOT4) = range(1, 15)
(MS_X, MS_MIXER, X_MIXED, MS_X_MIXED, PICKED_SCORES, MS_FINAL, RESULT) = range(1, 8)
PE_TURNED, PE_NORMS, PE_TURNED2, PE_PICKED = range(1, 5)
DVE_SCALED, DVE_X_LO, DVE_MIXED_LO, DVE_SCALED2, DVE_X2_LO, DVE_PICKED = 2, 3, 34, 36, 37, 64


def pool_splits(n):
    if n < CONV0:
        return n // 2 + 1
    if n < WOUT0:
        return CONV0 // 2 + (n - CONV0) + 1
    base = CONV0 // 2 + WOUT0 - CONV0
    if n < DOWN0:
        return base + (n - WOUT0) // 2 + 1
    base += (DOWN0 - WOUT0) // 2
    if n < PAIR0:
        return base + (n - DOWN0) + 1
    return base + EARLY + (n - PAIR0) // 2 + 1


def dve_splits(n):
    if n < CONV0:
        return n // 2 + 1
    if n < DOWN0:
        return CONV0 // 2 + (n - WOUT0) // 2 + 1
    base = CONV0 // 2 + (DOWN0 - WOUT0) // 2
    if n < MIXED_LO:
        return base + (n - PAIR0) // 2 + 1
    return base + (MIXED_LO - PAIR0) // 2 + (n - MIXED_LO) + 1


def split_by_pool(n):
    if CONV0 <= n < WOUT0 or DOWN0 <= n < PAIR0:
        return True
    return n < MIXED_LO and n % 2 == 0


def block_kernel(nc, x, stream, keys, columns, consts, final_g, out):
    f32, f32r, u32 = mybir.dt.float32, mybir.dt.float32r, mybir.dt.uint32
    ALU, ACT, AX = mybir.AluOpType, mybir.ActivationFunctionType, mybir.AxisListType
    ctx = ExitStack()
    with ctx:
        def sb(name, shape, dt=f32):
            return ctx.enter_context(nc.sbuf_tensor(name, shape, dt))

        def sem(name):
            return ctx.enter_context(nc.semaphore(name))

        big = sb("big", [P, NKEYS * T])
        experts = big[:, :].rearrange("p (i t) -> p i t", t=T)
        raw = sb("raw", [P, RING, D])
        hi = sb("hi", [P, RING, D], f32r)
        lo = sb("lo", [P, RING, D], f32r)
        act_hi = sb("act_hi", [P, KC, T], f32r)
        act_lo = sb("act_lo", [P, KC, T], f32r)
        gelu_ring = sb("gelu_ring", [P, 2, T])
        w_hi = sb("w_hi", [P, 2, T], f32r)
        w_lo = sb("w_lo", [P, 2, T], f32r)
        picked_T = sb("picked_T", [P, 3, T])
        ident = sb("ident", [P, P])
        iota = sb("iota", [P, P])
        cols = sb("cols", [P, 36])
        stats = sb("stats", [P, 48])

        def view(at, *shape):
            n = 1
            for s in shape:
                n *= s
            v = big[:, at:at + n]
            if len(shape) == 2:
                v = v.rearrange("p (a b) -> p a b", b=shape[1])
            if len(shape) == 3:
                v = v.rearrange("p (a b c) -> p a b c", b=shape[1], c=shape[2])
            return v

        qk_T = view(0, 8, T)
        v_sb = view(2048, TT, 512)
        mixer_T = view(3072, KC, T)
        mixed = view(5120, KC, T)
        masked = view(7168, 2, 384)
        probs = view(7936, 2, 384)
        probs_T = view(8704, 2, 384)
        consts_front = view(9472, 512)
        mask, ones = consts_front[:, 0:384], consts_front[:, 384:512]
        small = view(10240, 2048)
        query_T = view(12288, 16, T)
        c_gate = view(12288, 2, T)
        padded = view(12800, 2, T + 2)
        taps = view(13400, 2, 3, T)
        keys_sb = view(16384, 16, NKEYS)
        scores = view(18432, TT, 16, NKEYS)
        scores_left = view(22528, 16, NKEYS)
        first_index = view(22528, 16, TOPK)
        pairs = view(24576, PH, TOPK * TOPK)
        pairs_left = view(26624, PH, TOPK * TOPK)
        x_scaled = view(26624, TT, D)
        square_x = view(24576, TT, D)
        x_mixed = view(28672, TT, D)
        x_sb = view(30720, TT, D)
        lookup = view(30720, PH * TOPK, TOPK)
        mixer_sq = view(18432, KC, T)
        rstd_rows = view(20480, 2, T)
        top1 = small[:, 0:256].rearrange("p (h k) -> p h k", k=TOPK)
        top1_at = small[:, 256:512].bitcast(u32).rearrange("p (h k) -> p h k", k=TOPK)
        pos = small[:, 512:640].bitcast(u32)
        pos_ab = small[:, 640:896].bitcast(u32).rearrange("p (a k) -> p a k", a=2)
        ranks = small[:, 896:1152].rearrange("p (a k) -> p a k", a=2)
        picked = small[:, 1152:1920].rearrange("p (c t k) -> p c t k", c=3, t=TT)
        final_gain = view(0, D)
        result = view(D, TT, D)
        final_sq = view(3 * D, D)
        hot_i = raw[:, 0:2, :].rearrange("p a (b u n) -> p (a b) u n", b=2, u=QUAD)
        hot_j = raw[:, 2:4, :].rearrange("p a (b u n) -> p (a b) u n", b=2, u=QUAD)

        ms, root, rstd = stats[:, 0:2], stats[:, 2:4], stats[:, 4:6]
        sumsq = stats[:, 6:12].rearrange("p (a t) -> p a t", t=TT)
        neg_max = stats[:, 12:16].rearrange("p (a t) -> p a t", t=2)
        prob_sum = stats[:, 16:20].rearrange("p (a t) -> p a t", t=2)
        prob_inv = stats[:, 20:24].rearrange("p (a t) -> p a t", t=2)
        gate_sum = stats[:, 24:40]
        g_mix, g_out, g_ffn = cols[:, 0:8], cols[:, 8:16], cols[:, 16:24]
        conv_w = cols[:, 24:36].rearrange("p (c w) -> p c w", w=3)

        acc = ctx.enter_context(nc.psum_tensor("acc", [P, 4, 512], f32))
        proj = [ctx.enter_context(nc.psum_tensor(f"proj{b}", [P, 512], f32)) for b in range(2)]
        work = [ctx.enter_context(nc.psum_tensor(f"work{b}", [P, 512], f32)) for b in range(2)]

        def acc_view(k):
            return acc[:, k // 2, (k % 2) * T:(k % 2 + 1) * T]

        routed = [bank[:, :] for bank in work + proj]

        x_loaded = sem("x_loaded")
        consts_loaded = sem("consts_loaded")
        keys_loaded = sem("keys_loaded")
        gain_loaded = sem("gain_loaded")
        out_stored = sem("out_stored")
        raw_loaded = [sem(f"raw_loaded{s}") for s in range(RING)]
        hi_ready = sem("hi_ready")
        lo_by_pool = sem("lo_by_pool")
        lo_by_dve = sem("lo_by_dve")
        block_used = sem("block_used")
        proj_taken = sem("proj_taken")
        conv_taken = sem("conv_taken")
        act_step = sem("act_step")
        dve_step = sem("dve_step")
        pe_step = sem("pe_step")
        dve_ready = sem("dve_ready")
        scores_ready = sem("scores_ready")
        masked_ready = sem("masked_ready")
        exp_ready = sem("exp_ready")
        probs_ready = sem("probs_ready")
        turned_ready = sem("turned_ready")
        turned_taken = sem("turned_taken")
        head_ready = sem("head_ready")
        heads_taken = sem("heads_taken")
        c_taken = sem("c_taken")
        mixed_ready = sem("mixed_ready")
        key_scores = sem("key_scores")
        key_scores_taken = sem("key_scores_taken")
        topk_step = sem("topk_step")
        hot_ready = sem("hot_ready")
        hot_weighted = sem("hot_weighted")
        router_ready = sem("router_ready")
        router_act = sem("router_act")
        router_dve = sem("router_dve")
        w_ready = sem("w_ready")
        w_hi_ready = sem("w_hi_ready")
        w_lo_ready = sem("w_lo_ready")

        block = ctx.enter_context(nc.Block())

        def wait_low(eng, n):
            if split_by_pool(n):
                eng.wait_ge(lo_by_pool, pool_splits(n))
            else:
                eng.wait_ge(lo_by_dve, dve_splits(n))

        @block.sync
        def _(sp):
            def load(n, s):
                sp.dma_start(raw[:, s, :], stream[bass.ds(n, 1), :, :].rearrange("a p n -> (a p) n")
                             ).then_inc(raw_loaded[s], 16)

            def refill(first, last, waits):
                with sp.Fori(0, (last - first) // RING) as r:
                    for s in range(RING):
                        semaphore, start, step = waits(s)
                        sp.wait_ge(semaphore, r * step + start)
                        load(r * RING + (first + s), s)

            def taking_turns(first):
                def waits(s):
                    n = first - RING + s
                    if s % 2 == 0:
                        return lo_by_pool, pool_splits(n), 2
                    return lo_by_dve, dve_splits(n), 2
                return waits

            for t in range(TT):
                sp.dma_start(x_sb[:, t, :], x[t * P:(t + 1) * P, :]).then_inc(x_loaded, 16)
            for s in range(RING):
                load(s, s)
            refill(RING, CONV0 + RING, taking_turns(RING))
            refill(CONV0 + RING, WOUT0 + RING, lambda s: (lo_by_pool, pool_splits(CONV0 + s), RING))
            refill(WOUT0 + RING, DOWN0 + RING, taking_turns(WOUT0 + RING))
            refill(DOWN0 + RING, PAIR0, lambda s: (lo_by_pool, pool_splits(DOWN0 + s), RING))
            for s in range(2):
                wait_low(sp, PAIR0 - RING + s)
                load(PAIR0 + s, s)
            sp.wait_ge(router_ready, GROUPS)
            for s in (2, 3, 0, 1):
                load(PAIR0 + s if s >= 2 else PAIR0 + RING + s, s)
            for s in (2, 3):
                wait_low(sp, PAIR0 + s)
                load(PAIR0 + RING + s, s)
            refill(PAIR0 + 2 * RING, MIXED_LO + RING, taking_turns(PAIR0 + 2 * RING))
            refill(MIXED_LO + RING, BLOCKS, lambda s: (lo_by_dve, dve_splits(MIXED_LO + s), RING))
            sp.wait_ge(w_lo_ready, 16)
            sp.dma_start(final_gain, final_g.partition_broadcast(P)).then_inc(gain_loaded, 16)
            for t in range(TT):
                sp.wait_ge(dve_ready, RESULT + t)
                sp.dma_start(out[t * P:(t + 1) * P, :], result[:, t, :]).then_inc(out_stored, 16)
            sp.wait_ge(out_stored, 16 * TT)

        @block.gpsimd
        def _(pool):
            def split(n, s):
                pool.wait_ge(hi_ready, n + 1)
                pool.tensor_tensor(lo[:, s, :], raw[:, s, :], hi[:, s, :].bitcast(f32),
                                   ALU.subtract).then_inc(lo_by_pool, 1)

            def every_other(first, last):
                with pool.Fori(0, (last - first) // RING) as r:
                    for s in (0, 2):
                        split(r * RING + (first + s), s)

            def every(first, last):
                with pool.Fori(0, (last - first) // RING) as r:
                    for s in range(RING):
                        split(r * RING + (first + s), s)

            every_other(QK0, CONV0)
            every(CONV0, WOUT0)
            every_other(WOUT0, DOWN0)
            every(DOWN0, PAIR0)
            split(PAIR0, 0)
            pool.wait_ge(act_step, ACT_PICKED)
            with pool.Fori(0, GROUPS // RING) as r:
                for s in range(RING):
                    pool.wait_ge(hot_ready, r * RING + (s + 1))
                    weight = picked_T[:, 2, bass.ds(r * (RING * QUAD) + s * QUAD, QUAD)]
                    pool.tensor_tensor(hot_i[:, s], hot_i[:, s],
                                       weight.unsqueeze(2).to_broadcast([P, QUAD, NKEYS]),
                                       ALU.mult).then_inc(hot_weighted, 1)
            split(PAIR0 + 2, 2)
            every_other(PAIR0 + RING, MIXED_LO)

        @block.scalar
        def _(act):
            def high(n, s, m=None):
                act.wait_ge(raw_loaded[s], 16 * (n // RING + 1) if m is None else m)
                act.activation(hi[:, s, :], raw[:, s, :], ACT.Copy).then_inc(hi_ready, 1)

            def highs(first, r, s):
                high(None, s, r * 16 + 16 * (first // RING + 1))

            def root(ready, out_ap, in_ap):
                act.wait_ge(dve_ready, ready)
                act.activation(out_ap, in_ap, ACT.Sqrt).then_inc(act_step, 1)

            def sum_of_squares(source, which):
                for t in range(TT):
                    done = act.activation(square_x[:, t, :], source[:, t, :], ACT.Square,
                                          accum_out=sumsq[:, which, t:t + 1])
                done.then_inc(act_step, 1)

            def transposed_high(gains, step):
                act.wait_ge(pe_step, step)
                for k in range(KC):
                    done = act.activation(act_hi[:, k, :], acc_view(k), ACT.Copy, scale=gains[:, k:k + 1])
                done.then_inc(act_step, 1)

            act.dma_start(cols[:, :], columns).then_inc(consts_loaded, 16)
            act.dma_start(ident[:, :], consts[:, 0:128]).then_inc(consts_loaded, 16)
            act.dma_start(iota[:, :], consts[:, 128:256]).then_inc(consts_loaded, 16)
            act.dma_start(consts_front, consts[:, 256:768]).then_inc(consts_loaded, 16)
            act.dma_start(keys_sb, keys.rearrange("p (h n) -> p h n", n=NKEYS)).then_inc(keys_loaded, 16)
            act.wait_ge(x_loaded, 16 * TT)
            sum_of_squares(x_sb, 0)
            high(0, 0)
            high(1, 1)
            root(MS_X, stats[:, 2:4], ms)
            high(2, 2)
            high(3, 3)
            act.wait_ge(consts_loaded, 64)
            transposed_high(g_mix, PE_TURNED)
            with act.Fori(0, (V0 - QK0) // RING) as r:
                for s in range(RING):
                    act.wait_ge(block_used, r * RING + (s + 1))
                    act.activation(qk_T[:, bass.ds(r * RING + s, 1), :], proj[s % 2][:, 0:T].unsqueeze(1),
                                   ACT.Copy).then_inc(proj_taken, 1)
                    highs(RING, r, s)
            for n in range(V0, CONV0):
                act.wait_ge(block_used, n + 1)
                if n == CONV0 - 1:
                    act.activation(v_sb, acc[:, 0:2, :], ACT.Copy).then_inc(act_step, 1)
                high(n + RING, n % RING)
            for st in range(WOUT0 - CONV0):
                n, c = CONV0 + st, st // 3
                act.wait_ge(block_used, n + 1)
                if st % 3 == 0:
                    if c >= 2:
                        act.wait_ge(conv_taken, 2 * (c - 2) + 1)
                    act.activation(c_gate[:, c % 2, :], proj[n % 2][:, 0:T], ACT.Copy).then_inc(proj_taken, 1)
                if st < HEADS:
                    b = st % 2
                    act.wait_ge(masked_ready, st + 1)
                    if st >= 2:
                        act.wait_ge(turned_ready, st - 1)
                    act.activation(probs[:, b, 0:P], masked[:, b, 0:P], ACT.Exp,
                                   bias=neg_max[:, b, 0:1], accum_out=prob_sum[:, b, 0:1])
                    act.activation(probs[:, b, P:384], masked[:, b, P:384], ACT.Exp,
                                   bias=neg_max[:, b, 1:2], accum_out=prob_sum[:, b, 1:2]
                                   ).then_inc(exp_ready, 1)
                high(n + RING, n % RING)
                if 2 <= st < HEADS + 2:
                    h = st - 2
                    act.wait_ge(turned_ready, h + 1)
                    if h >= 2:
                        act.wait_ge(head_ready, h - 1)
                    act.activation(probs_T[:, h % 2, :], acc[:, 2 + h % 2, 0:384], ACT.Copy
                                   ).then_inc(turned_taken, 1)
                if 3 <= st < HEADS + 3 and st % 2 == 0:
                    h = st - 3
                    act.wait_ge(head_ready, h + 1)
                    act.activation(mixer_T[:, 4 + h // 2, :], acc[:, (h // 2) % 2, 0:T], ACT.Copy
                                   ).then_inc(heads_taken, 1)
            act.wait_ge(heads_taken, HEADS // 2)
            act.activation(mixer_sq[:, 4:8, :], mixer_T[:, 4:8, :], ACT.Square).then_inc(heads_taken, 1)
            act.wait_ge(conv_taken, 8)
            act.activation(mixer_sq[:, 0:4, :], mixer_T[:, 0:4, :], ACT.Square).then_inc(heads_taken, 1)
            root(MS_MIXER, rstd_rows, rstd_rows)
            for c in range(KC):
                act.wait_ge(mixed_ready, c + 1)
                done = act.activation(act_hi[:, c, :], mixed[:, c, :], ACT.Copy)
            done.then_inc(act_step, 1)
            with act.Fori(0, (WQ0 - WOUT0) // RING) as r:
                for s in range(RING):
                    act.wait_ge(block_used, r * RING + (WOUT0 + s + 1))
                    highs(WOUT0 + RING, r, s)
            act.wait_ge(dve_ready, X_MIXED)
            sum_of_squares(x_mixed, 1)
            root(MS_X_MIXED, stats[:, 2:4], ms)
            transposed_high(g_ffn, PE_TURNED2)
            with act.Fori(0, (DOWN0 - WQ0) // RING) as r:
                for s in range(RING):
                    act.wait_ge(block_used, r * RING + (WQ0 + s + 1))
                    act.activation(query_T[:, bass.ds(r * RING + s, 1), :], proj[s % 2][:, 0:T].unsqueeze(1),
                                   ACT.Copy).then_inc(proj_taken, 1)
                    highs(WQ0 + RING, r, s)
            for q in range(8):
                act.wait_ge(key_scores, q + 1)
                act.activation(scores[:, q // 4, 4 * (q % 4):4 * (q % 4) + 4, :],
                               work[q % 2][:, :].rearrange("p (h n) -> p h n", n=NKEYS),
                               ACT.Copy).then_inc(key_scores_taken, 1)
            act.preload_act_table(ACT.Gelu)
            with act.Fori(0, EARLY // RING - 1) as r:
                for s in range(RING):
                    act.wait_ge(block_used, r * RING + (DOWN0 + s + 1))
                    act.activation(experts[:, bass.ds(r * RING + s, 1), :], proj[s % 2][:, 0:T].unsqueeze(1),
                                   ACT.Gelu).then_inc(proj_taken, 1)
                    highs(DOWN0 + RING, r, s)
            for s in range(RING):
                i = EARLY - RING + s
                act.wait_ge(block_used, DOWN0 + i + 1)
                act.activation(experts[:, i, :], proj[s % 2][:, 0:T], ACT.Gelu).then_inc(proj_taken, 1)
                if s < 2:
                    high(PAIR0 + s, s)
            act.wait_ge(dve_ready, PICKED_SCORES)
            act.activation(picked[:, 2], picked[:, 2], ACT.Exp).then_inc(act_step, 1)
            act.wait_ge(pe_step, PE_PICKED)
            act.activation(picked_T[:, 0:2, :], work[0][:, :].rearrange("p (a t) -> p a t", t=T), ACT.Copy)
            act.activation(picked_T[:, 2, :], work[1][:, 0:T], ACT.Copy).then_inc(act_step, 1)
            with act.Fori(0, GROUPS // RING) as r:
                for s in range(RING):
                    act.wait_ge(router_ready, r * RING + (s + 1))
                    act.activation(experts[:, EARLY:NKEYS, bass.ds(r * (RING * QUAD) + s * QUAD, QUAD)]
                                   .rearrange("p i u -> p u i"),
                                   routed[s].rearrange("p (u i) -> p u i", i=NKEYS)[:, :, EARLY:NKEYS],
                                   ACT.Copy).then_inc(router_act, 1)

            def weight_high(m, b, ready):
                act.wait_ge(w_ready, ready)
                act.activation(w_hi[:, b, :].unsqueeze(1), experts[:, m, :], ACT.Copy).then_inc(w_hi_ready, 1)

            for b in range(2):
                weight_high(slice(b, b + 1), b, b + 1)
            for s in (2, 3):
                high(PAIR0 + s, s)
            act.preload_act_table(ACT.Gelu)
            with act.Fori(0, PAIRS // 2) as r:
                for b in range(2):
                    act.wait_ge(block_used, r * 4 + (PAIR0 + 2 * b + 1))
                    act.wait_ge(w_ready, r * 2 + (EARLY + b - 1))
                    act.activation(gelu_ring[:, b, :], proj[b][:, 0:T], ACT.Gelu).then_inc(proj_taken, 1)
                    highs(PAIR0 + RING, r, 2 * b)
                    act.wait_ge(block_used, r * 4 + (PAIR0 + 2 * b + 2))
                    weight_high(bass.ds(r * 2 + (b + 2), 1), b, r * 2 + (b + 3))
                    highs(PAIR0 + RING, r, 2 * b + 1)
            with act.Fori(0, EARLY // RING - 1) as r:
                for s in range(RING):
                    act.wait_ge(block_used, r * RING + (UP0 + s + 1))
                    weight_high(bass.ds(r * RING + (PAIRS + s + 2), 1), s % 2, r * RING + (PAIRS + s + 3))
                    highs(UP0 + RING, r, s)
            for s in range(2):
                m = NKEYS - 2 + s
                act.wait_ge(block_used, BLOCKS - RING + s + 1)
                weight_high(slice(m, m + 1), s, m + 1)
            act.wait_ge(block_used, BLOCKS)
            for t in range(TT):
                if t:
                    act.wait_ge(act_step, ACT_SUMSQ4 + t - 1)
                act.activation(final_sq, acc[:, 2 * t:2 * t + 2, :].rearrange("p a n -> p (a n)"),
                               ACT.Square, accum_out=sumsq[:, 2, t:t + 1]).then_inc(act_step, 1)
            root(MS_FINAL, stats[:, 2:4], ms)

        @block.vector
        def _(dve):
            chain = [0]

            def link(done):
                chain[0] += 1
                done.then_inc(dve_step, 1)
                dve.wait_ge(dve_step, chain[0])

            def low(n, s):
                dve.wait_ge(hi_ready, n + 1)
                dve.tensor_tensor(lo[:, s, :], raw[:, s, :], hi[:, s, :].bitcast(f32),
                                  ALU.subtract).then_inc(lo_by_dve, 1)

            def scaled(source, step):
                dve.wait_ge(act_step, step)
                link(dve.reciprocal(rstd, stats[:, 2:4]))
                for t in range(TT):
                    done = dve.tensor_scalar(x_scaled[:, t, :], source[:, t, :], rstd[:, t:t + 1], None, ALU.mult)
                link(done)

            def transposed_low(gains, step):
                dve.wait_ge(act_step, step)
                for k in range(KC):
                    done = dve.scalar_tensor_tensor(act_lo[:, k, :], acc_view(k), gains[:, k:k + 1],
                                                    act_hi[:, k, :].bitcast(f32), ALU.mult, ALU.subtract)
                link(done)

            dve.wait_ge(act_step, ACT_SUMSQ1)
            dve.tensor_scalar(ms, sumsq[:, 0, :], 1.0 / D, EPS, ALU.mult, ALU.add).then_inc(dve_ready, 1)
            low(1, 1)
            scaled(x_sb, ACT_ROOT1)
            assert chain[0] == DVE_SCALED, chain[0]
            low(3, 3)
            dve.memset(padded[:, :, 0:2], 0.0)
            transposed_low(g_mix, ACT_X_HI)
            assert chain[0] == DVE_X_LO, chain[0]
            for n in range(5, CONV0, 2):
                low(n, n % RING)
            for st in range(WOUT0 - CONV0 + 1):
                n, c = CONV0 + st, st // 3
                if 1 <= st <= HEADS:
                    h = st - 1
                    b = h % 2
                    dve.wait_ge(exp_ready, h + 1)
                    link(dve.reciprocal(prob_inv[:, b, :], prob_sum[:, b, :]))
                    dve.tensor_scalar(probs[:, b, 0:P], probs[:, b, 0:P], prob_inv[:, b, 0:1], None, ALU.mult)
                    dve.tensor_scalar(probs[:, b, P:384], probs[:, b, P:384], prob_inv[:, b, 1:2], None,
                                      ALU.mult).then_inc(probs_ready, 1)
                if st == WOUT0 - CONV0:
                    break
                if st % 3 == 1:
                    dve.wait_ge(proj_taken, 8 + c + 1)
                    dve.wait_ge(block_used, n + 1)
                    b = c % 2
                    done = dve.tensor_tensor(padded[:, b, 2:T + 2], proj[n % 2][:, 0:T], c_gate[:, b, :], ALU.mult)
                    done.then_inc(conv_taken, 1)
                    dve.wait_ge(conv_taken, 2 * c + 1)
                    link(dve.tensor_scalar(taps[:, b, 0, :], padded[:, b, 2:T + 2], conv_w[:, c, 2:3], None, ALU.mult))
                    link(dve.scalar_tensor_tensor(taps[:, b, 1, :], padded[:, b, 1:T + 1], conv_w[:, c, 1:2],
                                                  taps[:, b, 0, :], ALU.mult, ALU.add))
                    link(dve.scalar_tensor_tensor(taps[:, b, 2, :], padded[:, b, 0:T], conv_w[:, c, 0:1],
                                                  taps[:, b, 1, :], ALU.mult, ALU.add))
                if st % 3 == 2:
                    dve.wait_ge(block_used, n + 1)
                    dve.tensor_tensor(mixer_T[:, c, :], proj[n % 2][:, 0:T], taps[:, c % 2, 2, :],
                                      ALU.mult).then_inc(conv_taken, 1)
                if st < HEADS:
                    b = st % 2
                    dve.wait_ge(scores_ready, st + 1)
                    if st >= 2:
                        dve.wait_ge(exp_ready, st - 1)
                    link(dve.scalar_tensor_tensor(masked[:, b, :], work[b][:, 0:384], float(HD) ** -0.5,
                                                  mask, ALU.mult, ALU.add))
                    dve.reduce_max(neg_max[:, b, 0:1], masked[:, b, 0:P], AX.X, negate=True)
                    dve.reduce_max(neg_max[:, b, 1:2], masked[:, b, P:384], AX.X, negate=True
                                   ).then_inc(masked_ready, 1)
                if n + RING >= WOUT0 and n % 2:
                    low(n + RING, n % RING)
            dve.wait_ge(pe_step, PE_NORMS)
            link(dve.tensor_scalar(rstd_rows[:, 0, :], work[0][:, 0:T], 1.0 / 512, EPS, ALU.mult, ALU.add))
            dve.tensor_scalar(rstd_rows[:, 1, :], work[1][:, 0:T], 1.0 / 512, EPS, ALU.mult,
                              ALU.add).then_inc(dve_ready, 1)
            dve.wait_ge(act_step, ACT_ROOT2)
            link(dve.reciprocal(rstd_rows, rstd_rows))
            for c in range(KC):
                dve.scalar_tensor_tensor(mixed[:, c, :], mixer_T[:, c, :], g_out[:, c:c + 1],
                                         rstd_rows[:, c // 4, :], ALU.mult, ALU.mult).then_inc(mixed_ready, 1)
            dve.wait_ge(act_step, ACT_MIXED_HI)
            for c in range(KC):
                done = dve.tensor_tensor(act_lo[:, c, :], mixed[:, c, :], act_hi[:, c, :].bitcast(f32), ALU.subtract)
            link(done)
            assert chain[0] == DVE_MIXED_LO, chain[0]
            for n in range(WOUT0 + RING + 1, WQ0 + RING, 2):
                low(n, n % RING)
            dve.wait_ge(block_used, WQ0)
            for t in range(TT):
                done = dve.tensor_tensor(x_mixed[:, t, :].rearrange("p (a n) -> p a n", a=2),
                                         acc[:, 2 * t:2 * t + 2, :],
                                         x_sb[:, t, :].rearrange("p (a n) -> p a n", a=2), ALU.add)
            done.then_inc(dve_ready, 1)
            dve.wait_ge(act_step, ACT_SUMSQ3)
            dve.tensor_scalar(ms, sumsq[:, 1, :], 1.0 / D, EPS, ALU.mult, ALU.add).then_inc(dve_ready, 1)
            scaled(x_mixed, ACT_ROOT3)
            assert chain[0] == DVE_SCALED2, chain[0]
            transposed_low(g_ffn, ACT_X2_HI)
            assert chain[0] == DVE_X2_LO, chain[0]
            with dve.Fori(0, (DOWN0 - WQ0) // RING - 1) as r:
                for s in (1, 3):
                    low(r * RING + (WQ0 + RING + s), s)

            taken = [0]

            def step(done):
                taken[0] += 1
                done.then_inc(topk_step, 1)
                return taken[0]

            def top16(values, left, best, at, rows):
                first = [step(dve.max(best[:, h, 0:8], values[:, h, :])) for h in range(rows)]
                for h in range(rows):
                    dve.wait_ge(topk_step, first[h])
                    step(dve.max_index(at[:, h, 0:8], best[:, h, 0:8], values[:, h, :]))
                rest = []
                for h in range(rows):
                    rest.append(step(dve.match_replace(left[:, h, :], best[:, h, 0:8], values[:, h, :], LOWEST)))
                second = []
                for h in range(rows):
                    dve.wait_ge(topk_step, rest[h])
                    second.append(step(dve.max(best[:, h, 8:16], left[:, h, :])))
                for h in range(rows):
                    dve.wait_ge(topk_step, second[h])
                    last = step(dve.max_index(at[:, h, 8:16], best[:, h, 8:16], left[:, h, :]))
                dve.wait_ge(topk_step, last)

            for t in range(TT):
                dve.wait_ge(key_scores_taken, 4 * (t + 1))
                top16(scores[:, t], scores_left, top1, top1_at, 16)
                link(dve.tensor_copy(first_index, top1_at))
                halves = top1.rearrange("p (h a) k -> p h a k", a=2)
                link(dve.tensor_tensor(
                    pairs.rearrange("p h (a b) -> p h a b", b=TOPK),
                    halves[:, :, 0, :].unsqueeze(3).to_broadcast([P, PH, TOPK, TOPK]),
                    halves[:, :, 1, :].unsqueeze(2).to_broadcast([P, PH, TOPK, TOPK]), ALU.add))
                best = picked[:, 2, t, :].rearrange("p (h k) -> p h k", k=TOPK)
                top16(pairs, pairs_left, best, pos.rearrange("p (h k) -> p h k", k=TOPK), PH)
                dve.tensor_scalar(pos_ab[:, 0, :], pos, 4, None, ALU.logical_shift_right)
                link(dve.tensor_scalar(pos_ab[:, 1, :], pos, 15, None, ALU.bitwise_and))
                link(dve.tensor_copy(ranks, pos_ab))
                for a in range(2):
                    link(dve.tensor_tensor(lookup,
                                           iota[:, 0:TOPK].unsqueeze(1).to_broadcast([P, PH * TOPK, TOPK]),
                                           ranks[:, a, :].unsqueeze(2).to_broadcast([P, PH * TOPK, TOPK]),
                                           ALU.is_equal))
                    spread = lookup.rearrange("p (h k) a -> p h k a", k=TOPK)
                    number = first_index.rearrange("p (h a) k -> p h a k", a=2)[:, :, a, :]
                    link(dve.tensor_tensor(spread, spread,
                                           number.unsqueeze(2).to_broadcast([P, PH, TOPK, TOPK]), ALU.mult))
                    link(dve.reduce_sum(picked[:, a, t, :], lookup, AX.X))
                peak = stats[:, 40:48]
                link(dve.tensor_copy(peak, best[:, :, 0]))
                link(dve.tensor_tensor(best, best, peak.unsqueeze(2).to_broadcast([P, PH, TOPK]), ALU.subtract))
            dve.memset(gate_sum, 0.0).then_inc(dve_ready, 1)
            dve.wait_ge(dve_ready, PICKED_SCORES)
            dve.wait_ge(act_step, ACT_EXP)
            gates = picked[:, 2].rearrange("p t (h k) -> p (t h) k", k=TOPK)
            link(dve.reduce_sum(gate_sum, gates, AX.X))
            link(dve.reciprocal(gate_sum, gate_sum))
            link(dve.tensor_tensor(gates, gates, gate_sum.unsqueeze(2).to_broadcast([P, TT * PH, TOPK]), ALU.mult))
            assert chain[0] == DVE_PICKED, chain[0]

            def hots(g, s):
                def token(c):
                    return (picked_T[:, c, bass.ds(g * QUAD, QUAD)].unsqueeze(2)
                            .to_broadcast([P, QUAD, NKEYS]))
                numbers = iota[:, :].unsqueeze(1).to_broadcast([P, QUAD, NKEYS])
                dve.tensor_tensor(hot_j[:, s], numbers, token(1), ALU.is_equal)
                dve.tensor_tensor(hot_i[:, s], numbers, token(0), ALU.is_equal).then_inc(hot_ready, 1)

            def rows_in_place(g, s):
                dve.wait_ge(router_act, g + 1)
                rows = experts[:, 0:EARLY, bass.ds(g * QUAD, QUAD)].rearrange("p i u -> p u i")
                return dve.tensor_tensor(rows, routed[s].rearrange("p (u i) -> p u i", i=NKEYS)[:, :, 0:EARLY],
                                         rows, ALU.mult)

            dve.wait_ge(act_step, ACT_PICKED)
            low(PAIR0 + 1, 1)
            dve.wait_ge(lo_by_pool, pool_splits(PAIR0))
            dve.wait_ge(lo_by_dve, dve_splits(PAIR0 + 1))
            for s in range(RING):
                hots(s, s)
            with dve.Fori(0, GROUPS // RING - 1) as r:
                for s in range(RING):
                    rows_in_place(r * RING + s, s).then_inc(router_dve, 1)
                    hots(r * RING + (RING + s), s)
            for s in range(RING - 1):
                rows_in_place(GROUPS - RING + s, s).then_inc(router_dve, 1)
            rows_in_place(GROUPS - 1, RING - 1).then_inc(w_ready, EARLY)

            def weight_low(m, b, ready):
                dve.wait_ge(w_hi_ready, ready)
                dve.tensor_tensor(w_lo[:, b, :].unsqueeze(1), experts[:, m, :],
                                  w_hi[:, b, :].bitcast(f32).unsqueeze(1), ALU.subtract).then_inc(w_lo_ready, 1)

            dve.wait_ge(router_act, GROUPS)
            for b in range(2):
                weight_low(slice(b, b + 1), b, b + 1)
            low(PAIR0 + 3, 3)
            with dve.Fori(0, PAIRS // 2) as r:
                for b in range(2):
                    dve.wait_ge(proj_taken, r * 2 + (28 + EARLY + b + 1))
                    row = experts[:, bass.ds(r * 2 + (EARLY + b), 1), :]
                    dve.tensor_tensor(row, row, gelu_ring[:, b, :].unsqueeze(1), ALU.mult).then_inc(w_ready, 1)
                    weight_low(bass.ds(r * 2 + (b + 2), 1), b, r * 2 + (b + 3))
                    low(r * RING + (PAIR0 + RING + 2 * b + 1), 2 * b + 1)
            with dve.Fori(0, EARLY // RING - 1) as r:
                for s in range(RING):
                    weight_low(bass.ds(r * RING + (PAIRS + s + 2), 1), s % 2, r * RING + (PAIRS + s + 3))
                    low(r * RING + (UP0 + RING + s), s)
            for s in range(2):
                m = NKEYS - 2 + s
                weight_low(slice(m, m + 1), s, m + 1)

            dve.wait_ge(act_step, ACT_SUMSQ4 + 1)
            dve.tensor_scalar(ms, sumsq[:, 2, :], 1.0 / D, EPS, ALU.mult, ALU.add).then_inc(dve_ready, 1)
            dve.wait_ge(act_step, ACT_ROOT4)
            link(dve.reciprocal(rstd, stats[:, 2:4]))
            dve.wait_ge(gain_loaded, 16)
            for t in range(TT):
                dve.scalar_tensor_tensor(result[:, t, :], acc[:, 2 * t:2 * t + 2, :].rearrange("p a n -> p (a n)"),
                                         rstd[:, t:t + 1], final_gain, ALU.mult, ALU.mult).then_inc(dve_ready, 1)

        @block.tensor
        def _(pe):
            def rows_product(s, target, first=True, last=True):
                for k in range(KC):
                    part = slice(k * P, (k + 1) * P)
                    pe.matmul(target, hi[:, s, part], act_hi[:, k, :], start=(k == 0), stop=False)
                    pe.matmul(target, hi[:, s, part], act_lo[:, k, :], start=False, stop=False)
                    done = pe.matmul(target, lo[:, s, part], act_hi[:, k, :], start=False, stop=(k == KC - 1))
                return done

            def token_product(left_hi, left_lo, right, target, width, start, stop):
                for t in range(TT):
                    part = slice(t * P, (t + 1) * P)
                    for left, rights in ((left_hi, (hi, lo)), (left_lo, (hi,))):
                        for r in rights:
                            for half in range(width):
                                done = pe.matmul(target(t, half), left[:, part], right(r, half),
                                                 start=start and left is left_hi and r is hi,
                                                 stop=stop and left is left_lo)
                return done

            def transposes(step, seen):
                pe.wait_ge(dve_step, seen)
                for k in range(KC):
                    for t in range(TT):
                        done = pe.transpose(acc_view(k)[:, t * P:(t + 1) * P],
                                            x_scaled[:, t, k * P:(k + 1) * P], ident[:, :])
                done.then_inc(pe_step, 1)

            pe.wait_ge(consts_loaded, 64)
            transposes(PE_TURNED, DVE_SCALED)
            pe.wait_ge(dve_step, DVE_X_LO)
            for n in range(QK0, V0):
                wait_low(pe, n)
                if n >= 2:
                    pe.wait_ge(proj_taken, n - 1)
                rows_product(n % RING, proj[n % 2][:, 0:T]).then_inc(block_used, 1)
            for n in range(V0, CONV0):
                wait_low(pe, n)
                s = n % RING
                for c in range(2):
                    k = 2 * (n - V0) + c
                    done = token_product(act_hi[:, k, :], act_lo[:, k, :],
                                         lambda r, half: r[:, s, c * 512:(c + 1) * 512],
                                         lambda t, half: acc[:, t, :], 1, k == 0, k == KC - 1)
                done.then_inc(block_used, 1)
            for st in range(WOUT0 - CONV0):
                n, c = CONV0 + st, st // 3
                wait_low(pe, n)
                if st >= 2:
                    before = st - 2
                    if before % 3 == 0:
                        pe.wait_ge(proj_taken, 8 + before // 3 + 1)
                    else:
                        pe.wait_ge(conv_taken, 2 * (before // 3) + before % 3)
                else:
                    pe.wait_ge(proj_taken, 8)
                rows_product(n % RING, proj[n % 2][:, 0:T]).then_inc(block_used, 1)
                if st < HEADS:
                    if st >= 2:
                        pe.wait_ge(masked_ready, st - 1)
                    rows = slice(HD * (st % 2), HD * (st % 2) + HD)
                    q, k = qk_T[rows, st // 2, :], qk_T[rows, 4 + st // 2, :]
                    pe.matmul(work[st % 2][:, 0:P], q[:, 0:P], k[:, 0:P], start=True, stop=True)
                    pe.matmul(work[st % 2][:, P:384], q[:, P:T], k, start=True, stop=True
                              ).then_inc(scores_ready, 1)
                if 2 <= st < HEADS + 2:
                    h = st - 2
                    pe.wait_ge(probs_ready, h + 1)
                    if h >= 2:
                        pe.wait_ge(turned_taken, h - 1)
                    for b in range(3):
                        done = pe.transpose(acc[:, 2 + h % 2, b * P:(b + 1) * P],
                                            probs[:, h % 2, b * P:(b + 1) * P], ident[:, :])
                    done.then_inc(turned_ready, 1)
                if 3 <= st < HEADS + 3:
                    h = st - 3
                    pe.wait_ge(turned_taken, h + 1)
                    if h == 0:
                        pe.wait_ge(act_step, ACT_V)
                    if h >= 4 and h % 2 == 0:
                        pe.wait_ge(heads_taken, h // 2 - 1)
                    rows = slice(HD * (h % 2), HD * (h % 2) + HD)
                    target = acc[rows, (h // 2) % 2, :]
                    vh = v_sb[:, :, h * HD:(h + 1) * HD]
                    pe.matmul(target[:, 0:P], vh[:, 0, :], probs_T[:, h % 2, 0:P], start=True, stop=True)
                    pe.matmul(target[:, P:T], vh[:, 0, :], probs_T[:, h % 2, P:2 * P], start=True, stop=False)
                    pe.matmul(target[:, P:T], vh[:, 1, :], probs_T[:, h % 2, 2 * P:384], start=False,
                              stop=True).then_inc(head_ready, 1)
            for half, ready in ((1, HEADS // 2 + 1), (0, HEADS // 2 + 2)):
                pe.wait_ge(heads_taken, ready)
                for c in range(4):
                    done = pe.matmul(work[half][:, 0:T], ones, mixer_sq[:, 4 * half + c, :],
                                     start=(c == 0), stop=(c == 3))
            done.then_inc(pe_step, 1)
            pe.wait_ge(dve_step, DVE_MIXED_LO)
            for n in range(WOUT0, WQ0):
                wait_low(pe, n)
                s, c = n % RING, n - WOUT0
                token_product(act_hi[:, c, :], act_lo[:, c, :],
                              lambda r, half: r[:, s, half * 512:(half + 1) * 512],
                              lambda t, half: acc[:, 2 * t + half, :], 2, c == 0, c == KC - 1
                              ).then_inc(block_used, 1)
            transposes(PE_TURNED2, DVE_SCALED2)
            pe.wait_ge(dve_step, DVE_X2_LO)
            for t in range(TT):
                for half in range(2):
                    pe.matmul(acc[:, 2 * t + half, :], ident[:, :], x_mixed[:, t, half * 512:(half + 1) * 512],
                              start=True, stop=False)
            with pe.Fori(0, (DOWN0 - WQ0) // RING) as r:
                for s in range(RING):
                    by_pool = s % 2 == 0
                    pe.wait_ge(lo_by_pool if by_pool else lo_by_dve,
                               r * 2 + (pool_splits if by_pool else dve_splits)(WQ0 + s))
                    pe.wait_ge(proj_taken, r * RING + (12 + s - 1))
                    rows_product(s, proj[s % 2][:, 0:T]).then_inc(block_used, 1)
            pe.wait_ge(keys_loaded, 16)
            pe.wait_ge(proj_taken, 28)
            for q in range(8):
                if q >= 2:
                    pe.wait_ge(key_scores_taken, q - 1)
                for h in range(4):
                    row = 4 * (q % 4) + h
                    done = pe.matmul(work[q % 2][:, h * NKEYS:(h + 1) * NKEYS],
                                     query_T[:, row, (q // 4) * P:(q // 4 + 1) * P], keys_sb[:, row, :],
                                     start=True, stop=True)
                done.then_inc(key_scores, 1)
            with pe.Fori(0, EARLY // RING) as r:
                for s in range(RING):
                    pe.wait_ge(lo_by_pool, r * RING + pool_splits(DOWN0 + s))
                    pe.wait_ge(proj_taken, r * RING + (28 + s - 1))
                    rows_product(s, proj[s % 2][:, 0:T]).then_inc(block_used, 1)
            pe.wait_ge(dve_step, DVE_PICKED)
            pe.wait_ge(key_scores_taken, 8)
            for c in range(3):
                for t in range(TT):
                    at = (2 * c + t) % 4
                    done = pe.transpose(work[c // 2][:, at * P:(at + 1) * P], picked[:, c, t, :], ident[:, :])
            done.then_inc(pe_step, 1)

            def router(s):
                for u in range(QUAD):
                    done = pe.matmul(routed[s][:, u * NKEYS:(u + 1) * NKEYS], hot_j[:, s, u, :], hot_i[:, s, u, :],
                                     start=True, stop=True)
                done.then_inc(router_ready, 1)

            for g in range(RING):
                pe.wait_ge(hot_weighted, g + 1)
                if g < 2:
                    pe.wait_ge(act_step, ACT_PICKED)
                else:
                    pe.wait_ge(proj_taken, 28 + EARLY)
                router(g)
            with pe.Fori(0, GROUPS // RING - 1) as r:
                for s in range(RING):
                    pe.wait_ge(hot_weighted, r * RING + (RING + s + 1))
                    pe.wait_ge(router_dve, r * RING + (s + 1))
                    router(s)

            def up(s, b, stop):
                return token_product(w_hi[:, b, :], w_lo[:, b, :],
                                     lambda r, half: r[:, s, half * 512:(half + 1) * 512],
                                     lambda t, half: acc[:, 2 * t + half, :], 2, False, stop)

            pe.wait_ge(w_ready, EARLY)
            with pe.Fori(0, PAIRS // 2) as r:
                for b in range(2):
                    pe.wait_ge(lo_by_pool, r * 2 + pool_splits(PAIR0 + 2 * b))
                    pe.wait_ge(proj_taken, r * 2 + (28 + EARLY + b - 1))
                    rows_product(2 * b, proj[b][:, 0:T]).then_inc(block_used, 1)
                    pe.wait_ge(lo_by_dve, r * 2 + dve_splits(PAIR0 + 2 * b + 1))
                    pe.wait_ge(w_lo_ready, r * 2 + (b + 1))
                    up(2 * b + 1, b, False).then_inc(block_used, 1)
            for s in range(RING):
                wait_low(pe, UP0 + s)
                pe.wait_ge(w_lo_ready, PAIRS + s + 1)
                up(s, s % 2, False).then_inc(block_used, 1)
            with pe.Fori(0, EARLY // RING - 2) as r:
                for s in range(RING):
                    pe.wait_ge(lo_by_dve, r * RING + dve_splits(MIXED_LO + s))
                    pe.wait_ge(w_lo_ready, r * RING + (PAIRS + RING + s + 1))
                    up(s, s % 2, False).then_inc(block_used, 1)
            for s in range(RING):
                wait_low(pe, BLOCKS - RING + s)
                pe.wait_ge(w_lo_ready, NKEYS - RING + s + 1)
                up(s, s % 2, s == RING - 1).then_inc(block_used, 1)


def columns_of(w, first, count):
    part = w[:, first:first + count * P].reshape(KC, P, count, P)
    return part.transpose(2, 1, 0, 3).reshape(count, P, D)


def kernel(x, norm_mix_g, w_in, conv_w, norm_conv_out_g, norm_attn_out_g, w_out, norm_ffn_g, peer_w_query,
           peer_sub_keys1, peer_sub_keys2, peer_down, peer_up, final_norm_g):
    import numpy as np
    import concourse.bacc as bacc
    from concourse.bass_utils import run_bass_kernel_spmd

    w_in, w_out, wq = np.asarray(w_in)[0], np.asarray(w_out)[0], np.asarray(peer_w_query)[0]
    down, up = np.asarray(peer_down)[0], np.asarray(peer_up)[0]
    b_cols, c_cols, h_cols = (columns_of(w_in, 512 * g, 4) for g in range(3))
    down = down.reshape(NKEYS, NKEYS, KC, P).transpose(0, 3, 2, 1).reshape(NKEYS, P, D)
    up = up.reshape(NKEYS, NKEYS, D)
    parts = [
        columns_of(w_in, 1536, 8),
        w_in[:, 2560:3072].reshape(4, 2, P, 512).transpose(0, 2, 1, 3).reshape(4, P, D),
        np.stack([g[c] for c in range(4) for g in (c_cols, h_cols, b_cols)]),
        w_out.reshape(KC, P, D),
        columns_of(wq, 0, 16),
        down[:EARLY],
        np.stack([down[EARLY:], up[:PAIRS]], axis=1).reshape(2 * PAIRS, P, D),
        up[PAIRS:],
    ]
    stream = np.concatenate(parts)
    keys = np.stack([np.asarray(peer_sub_keys1)[0], np.asarray(peer_sub_keys2)[0]], axis=1)
    keys = np.ascontiguousarray(keys.transpose(3, 0, 1, 2).reshape(P, 2 * PH * NKEYS))

    def column(g):
        return np.asarray(g).reshape(-1, P).T

    taps = np.asarray(conv_w)[0].reshape(3, 4, P).transpose(2, 1, 0).reshape(P, 12)
    columns = np.ascontiguousarray(np.concatenate(
        [column(norm_mix_g[0]), column(norm_conv_out_g[0]), column(norm_attn_out_g[0]), column(norm_ffn_g[0]), taps],
        axis=1))
    n = np.arange(P)
    future = np.where(n[None, :] > n[:, None], NEG, 0.0)
    consts = np.concatenate([np.eye(P), np.tile(n, (P, 1)), future, np.zeros((P, P)), future, np.ones((P, P))],
                            axis=1).astype(np.float32)
    arrays = {
        "x": np.ascontiguousarray(np.asarray(x)[0]), "stream": stream, "keys": keys, "columns": columns,
        "consts": consts, "final_g": np.asarray(final_norm_g),
    }
    nc = bacc.Bacc("TRN2", target_bir_lowering=False, num_devices=1)
    args = [nc.dram_tensor(f"in_{k}", a.shape, mybir.dt.from_np(a.dtype), kind="ExternalInput").ap()
            for k, a in arrays.items()]
    args.append(nc.dram_tensor("out_x", (T, D), mybir.dt.float32, kind="ExternalOutput").ap())
    block_kernel(nc, *args)
    r = run_bass_kernel_spmd(nc, [{f"in_{k}": a for k, a in arrays.items()}], core_ids=[0])
    return r.results[0]["out_x"].reshape(1, T, D)
```

```python
import concourse.bass as bass
from concourse import mybir
from contextlib import ExitStack

P = 128
T = 256
TT = T // P
D = 1024
KC = D // P
HEADS, HD = 8, 64
NKEYS = 128
PH, TOPK = 8, 16
EPS = 1e-6
NEG = -1e30
LOWEST = -3.4e38

QK0, V0, CONV0, WOUT0, WQ0, DOWN0 = 0, 8, 12, 24, 32, 48
EARLY = 32
HELD = 8
AHEAD = EARLY + HELD
HELD0 = DOWN0 + EARLY
PAIR0 = DOWN0 + AHEAD
PAIRS = NKEYS - AHEAD
UP0 = PAIR0 + 2 * PAIRS
BLOCKS = UP0 + AHEAD
RING = 4
POOL0 = WQ0 + RING
MIXED_LO = UP0 + RING
QUAD = 4
GROUPS = T // QUAD
SPAN = GROUPS // HELD

(ACT_SUMSQ1, ACT_ROOT1, ACT_V, ACT_ROOT2, ACT_SUMSQ3, ACT_ROOT3, ACT_EXP, ACT_PICKED) = range(1, 9)
(MS_X, MS_MIXER, X_MIXED, X_MIXED_B, MS_X_MIXED, PICKED_SCORES) = range(1, 7)
SPLIT_X, SPLIT_MIXER, SPLIT_X_MIXED = 0, 4, 12
PE_NORMS, PE_PICKED = range(1, 3)
DVE_SCALED, DVE_SCALED2, DVE_PICKED = 2, 34, 61


def split_by_pool(n):
    if CONV0 <= n < WOUT0 or POOL0 <= n < PAIR0:
        return True
    return n < MIXED_LO and n % 2 == 0


POOL_SPLITS = [sum(split_by_pool(m) for m in range(n + 1)) for n in range(BLOCKS)]


def pool_splits(n):
    return POOL_SPLITS[n]


def raw_use(n):
    if n < HELD0:
        return n // RING + 1
    if n < PAIR0:
        return HELD0 // RING + (n - HELD0) // 2 + 1
    return HELD0 // RING + (HELD // 2 if n % RING < 2 else 0) + (n - PAIR0) // RING + 1


def dve_splits(n):
    return n + 1 - POOL_SPLITS[n]


def block_kernel(nc, x, stream, keys, columns, consts, final_g, x_mixed_dram, out):
    f32, f32r, u32 = mybir.dt.float32, mybir.dt.float32r, mybir.dt.uint32
    ALU, ACT, AX = mybir.AluOpType, mybir.ActivationFunctionType, mybir.AxisListType
    ctx = ExitStack()
    with ctx:
        def sb(name, shape, dt=f32):
            return ctx.enter_context(nc.sbuf_tensor(name, shape, dt))

        def sem(name):
            return ctx.enter_context(nc.semaphore(name))

        big = sb("big", [P, NKEYS * T])
        experts = big[:, :].rearrange("p (i t) -> p i t", t=T)
        raw = sb("raw", [P, RING, D])
        hi = sb("hi", [P, RING, D], f32r)
        lo = sb("lo", [P, RING, D], f32r)
        act_hi = sb("act_hi", [P, KC, T], f32r)
        act_lo = sb("act_lo", [P, KC, T], f32r)
        gelu_ring = sb("gelu_ring", [P, 2, T])
        w_hi = sb("w_hi", [P, 2, T], f32r)
        w_lo = sb("w_lo", [P, 2, T], f32r)
        picked_T = sb("picked_T", [P, 3, T])
        hot_more = sb("hot_more", [P, 2, QUAD, P])
        ident = sb("ident", [P, P])
        iota = sb("iota", [P, P])
        cols = sb("cols", [P, 36])
        stats = sb("stats", [P, 48])

        def view(at, *shape):
            n = 1
            for s in shape:
                n *= s
            v = big[:, at:at + n]
            if len(shape) == 2:
                v = v.rearrange("p (a b) -> p a b", b=shape[1])
            if len(shape) == 3:
                v = v.rearrange("p (a b c) -> p a b c", b=shape[1], c=shape[2])
            return v

        qk_T = view(0, 8, T)
        v_sb = view(2048, TT, 512)
        mixer_T = view(3072, KC, T)
        mixed = view(5120, KC, T)
        masked = view(7168, 2, 384)
        probs = view(7936, 2, 384)
        probs_T = view(8704, 2, 384)
        consts_front = view(9472, 512)
        mask, ones = consts_front[:, 0:384], consts_front[:, 384:512]
        small = view(10240, 2048)
        query_T = view(12288, 16, T)
        c_gate = view(12288, 2, T)
        padded = view(12800, 2, T + 2)
        taps = view(13400, 2, 3, T)
        keys_sb = view(16384, 16, NKEYS)
        scores = view(18432, TT, 16, NKEYS)
        scores_left = view(22528, 4, NKEYS)
        first_index = view(23040, 16, TOPK)
        pos_ab = view(23296, 2, P).bitcast(u32)
        ranks = view(23552, 2, P)
        pairs = view(24576, PH, TOPK * TOPK)
        pairs_left = view(26624, PH, TOPK * TOPK)
        x_scaled = view(26624, TT, D)
        square_x = view(24576, TT, D)
        x_mixed = view(28672, TT, D)
        x_sb = view(30720, TT, D)
        lookup = view(30720, PH * TOPK, TOPK)
        mixer_sq = view(18432, KC, T)
        rstd_rows = view(20480, 2, T)
        top1 = small[:, 0:512].rearrange("p (t h k) -> p t h k", t=TT, k=TOPK)
        top1_at = small[:, 512:1024].bitcast(u32).rearrange("p (t h k) -> p t h k", t=TT, k=TOPK)
        pos = small[:, 1024:1152].bitcast(u32)
        picked = small[:, 1152:1920].rearrange("p (c t k) -> p c t k", c=3, t=TT)
        final_gain = view(0, D)
        result = view(D, TT, D)
        final_sq = [view(3 * D, D), view(4 * D, D)]
        x_again = view(20 * T, TT, D)
        hot_i = raw[:, 2:4, :].rearrange("p a (b u n) -> p (a b) u n", b=2, u=QUAD)
        hot_j = [w.rearrange("p a (u n) -> p (a u) n", n=NKEYS) for w in (w_hi[:, :, :], w_lo[:, :, :])]
        hot_j += [hot_more[:, b] for b in range(2)]

        ms, root, rstd = stats[:, 0:2], stats[:, 2:4], stats[:, 4:6]
        sumsq = stats[:, 6:12].rearrange("p (a t) -> p a t", t=TT)
        neg_max = stats[:, 12:16].rearrange("p (a t) -> p a t", t=2)
        prob_sum = stats[:, 16:20].rearrange("p (a t) -> p a t", t=2)
        prob_inv = stats[:, 20:24].rearrange("p (a t) -> p a t", t=2)
        gate_sum = stats[:, 24:40]
        g_mix, g_out, g_ffn = cols[:, 0:8], cols[:, 8:16], cols[:, 16:24]
        conv_w = cols[:, 24:36].rearrange("p (c w) -> p c w", w=3)

        acc = ctx.enter_context(nc.psum_tensor("acc", [P, 4, 512], f32))
        proj = [ctx.enter_context(nc.psum_tensor(f"proj{b}", [P, 512], f32)) for b in range(2)]
        work = [ctx.enter_context(nc.psum_tensor(f"work{b}", [P, 512], f32)) for b in range(2)]

        def acc_view(k):
            return acc[:, k // 2, (k % 2) * T:(k % 2 + 1) * T]

        routed = [bank[:, :] for bank in work + proj]

        x_spilled = sem("x_spilled")
        x_reloaded = sem("x_reloaded")
        turned = sem("turned")
        x_loaded = [sem(f"x_loaded{t}") for t in range(TT)]
        consts_loaded = sem("consts_loaded")
        keys_loaded = sem("keys_loaded")
        gain_loaded = sem("gain_loaded")
        out_stored = sem("out_stored")
        raw_loaded = [sem(f"raw_loaded{s}") for s in range(RING)]
        hi_ready = sem("hi_ready")
        lo_by_pool = sem("lo_by_pool")
        lo_by_dve = sem("lo_by_dve")
        block_used = sem("block_used")
        proj_taken = sem("proj_taken")
        conv_taken = sem("conv_taken")
        act_step = sem("act_step")
        dve_step = sem("dve_step")
        pe_step = sem("pe_step")
        dve_ready = sem("dve_ready")
        scores_ready = sem("scores_ready")
        masked_ready = sem("masked_ready")
        exp_ready = sem("exp_ready")
        probs_ready = sem("probs_ready")
        turned_ready = sem("turned_ready")
        turned_taken = sem("turned_taken")
        head_ready = sem("head_ready")
        heads_taken = sem("heads_taken")
        c_taken = sem("c_taken")
        conv_squared = sem("conv_squared")
        mixed_ready = sem("mixed_ready")
        act_high = sem("act_high")
        act_split = sem("act_split")
        total_ready = sem("total_ready")
        final_sum = sem("final_sum")
        final_ms = sem("final_ms")
        final_root = sem("final_root")
        result_ready = sem("result_ready")
        key_scores = sem("key_scores")
        key_scores_taken = sem("key_scores_taken")
        topk_step = sem("topk_step")
        hot_ready = sem("hot_ready")
        hot_weighted = sem("hot_weighted")
        router_ready = sem("router_ready")
        router_act = sem("router_act")
        w_ready = sem("w_ready")
        w_hi_ready = sem("w_hi_ready")
        w_lo_ready = sem("w_lo_ready")

        block = ctx.enter_context(nc.Block())

        def wait_low(eng, n):
            if split_by_pool(n):
                eng.wait_ge(lo_by_pool, pool_splits(n))
            else:
                eng.wait_ge(lo_by_dve, dve_splits(n))

        @block.sync
        def _(sp):
            def load(n, s):
                sp.dma_start(raw[:, s, :], stream[bass.ds(n, 1), :, :].rearrange("a p n -> (a p) n")
                             ).then_inc(raw_loaded[s], 16)

            def refill(first, last, waits):
                with sp.Fori(0, (last - first) // RING) as r:
                    for s in range(RING):
                        semaphore, start, step = waits(s)
                        sp.wait_ge(semaphore, r * step + start)
                        load(r * RING + (first + s), s)

            def taking_turns(first):
                def waits(s):
                    n = first - RING + s
                    if s % 2 == 0:
                        return lo_by_pool, pool_splits(n), 2
                    return lo_by_dve, dve_splits(n), 2
                return waits

            for t in range(TT):
                sp.dma_start(x_sb[:, t, :], x[t * P:(t + 1) * P, :]).then_inc(x_loaded[t], 16)
            for s in range(RING):
                load(s, s)
            sp.dma_start(keys_sb, keys.rearrange("p (h n) -> p h n", n=NKEYS)).then_inc(keys_loaded, 16)
            refill(RING, CONV0 + RING, taking_turns(RING))
            refill(CONV0 + RING, WOUT0 + RING, lambda s: (lo_by_pool, pool_splits(CONV0 + s), RING))
            refill(WOUT0 + RING, POOL0 + RING, taking_turns(WOUT0 + RING))
            refill(POOL0 + RING, HELD0, lambda s: (lo_by_pool, pool_splits(POOL0 + s), RING))
            for s in range(2):
                wait_low(sp, HELD0 - RING + s)
                load(HELD0 + s, s)
            for n in range(HELD0 + 2, PAIR0 + 2):
                wait_low(sp, n - 2)
                load(n, n % 2)
            sp.wait_ge(router_ready, GROUPS)
            for s in (2, 3):
                load(PAIR0 + s, s)
            refill(PAIR0 + RING, MIXED_LO + RING, taking_turns(PAIR0 + RING))
            rest = BLOCKS - 2 * RING

            def by_dve(first):
                return lambda s: (lo_by_dve, dve_splits(first - RING + s), RING)
            refill(MIXED_LO + RING, rest, by_dve(MIXED_LO + RING))
            sp.wait_ge(w_lo_ready, 28)
            sp.dma_start(final_gain, final_g.partition_broadcast(P)).then_inc(gain_loaded, 16)
            sp.dma_start(x_again, x_mixed_dram.rearrange("(t p) n -> p t n", p=P)).then_inc(x_reloaded, 16)
            refill(rest, BLOCKS, by_dve(rest))
            for t in range(TT):
                sp.wait_ge(result_ready, t + 1)
                sp.dma_start(out[t * P:(t + 1) * P, :], result[:, t, :]).then_inc(out_stored, 16)
            sp.wait_ge(out_stored, 16 * TT)

        @block.gpsimd
        def _(pool):
            def split(n, s, raw_slot=None):
                pool.wait_ge(hi_ready, n + 1)
                pool.tensor_tensor(lo[:, s, :], raw[:, s if raw_slot is None else raw_slot, :], hi[:, s, :].bitcast(f32),
                                   ALU.subtract).then_inc(lo_by_pool, 1)

            def every_other(first, last):
                with pool.Fori(0, (last - first) // RING) as r:
                    for s in (0, 2):
                        split(r * RING + (first + s), s)

            def every(first, last):
                with pool.Fori(0, (last - first) // RING) as r:
                    for s in range(RING):
                        split(r * RING + (first + s), s)

            every_other(QK0, CONV0)
            every(CONV0, WOUT0)
            every_other(WOUT0, POOL0)
            every(POOL0, HELD0)
            split(HELD0, 0)
            pool.wait_ge(act_step, ACT_PICKED)
            with pool.Fori(0, HELD // RING) as r:
                for b in range(RING):
                    for g in range(SPAN):
                        at = RING * SPAN * r + (b * SPAN + g)
                        pool.wait_ge(hot_ready, at + 1)
                        weight = picked_T[:, 2, bass.ds(at * QUAD, QUAD)]
                        pool.tensor_tensor(hot_i[:, g % RING], hot_i[:, g % RING],
                                           weight.unsqueeze(2).to_broadcast([P, QUAD, NKEYS]),
                                           ALU.mult).then_inc(hot_weighted, 1)
                        if g == SPAN // 2 - 1:
                            split(r * RING + (HELD0 + b + 1), (b + 1) % RING, (b + 1) % 2)
            split(PAIR0 + 2, 2)
            every_other(PAIR0 + RING, MIXED_LO)

        @block.scalar
        def _(act):
            def high(n, s, loaded=None, raw_slot=None):
                raw_slot = s if raw_slot is None else raw_slot
                act.wait_ge(raw_loaded[raw_slot], 16 * raw_use(n) if loaded is None else loaded)
                act.activation(hi[:, s, :], raw[:, raw_slot, :], ACT.Copy).then_inc(hi_ready, 1)

            def highs(first, r, s):
                high(None, s, r * 16 + 16 * raw_use(first + s))

            def root(ready, out_ap, in_ap):
                act.wait_ge(dve_ready, ready)
                act.activation(out_ap, in_ap, ACT.Sqrt).then_inc(act_step, 1)

            def sum_of_squares(source, which, waits):
                for t in range(TT):
                    act.wait_ge(*waits[t])
                    done = act.activation(square_x[:, t, :], source[:, t, :], ACT.Square,
                                          accum_out=sumsq[:, which, t:t + 1])
                done.then_inc(act_step, 1)

            def transposed_high(gains, first):
                for k in range(KC):
                    act.wait_ge(turned, first + k // 2 + 1)
                    done = act.activation(act_hi[:, k, :], acc_view(k), ACT.Copy, scale=gains[:, k:k + 1])
                    if k % 2:
                        done.then_inc(act_high, 1)

            act.dma_start(cols[:, :], columns).then_inc(consts_loaded, 16)
            act.dma_start(ident[:, :], consts[:, 0:128]).then_inc(consts_loaded, 16)
            act.dma_start(iota[:, :], consts[:, 128:256]).then_inc(consts_loaded, 16)
            act.dma_start(consts_front, consts[:, 256:768]).then_inc(consts_loaded, 16)
            act.preload_act_table(ACT.Sqrt)
            sum_of_squares(x_sb, 0, [(x_loaded[t], 16) for t in range(TT)])
            root(MS_X, stats[:, 2:4], ms)
            high(0, 0)
            high(1, 1)
            high(2, 2)
            high(3, 3)
            act.wait_ge(consts_loaded, 64)
            transposed_high(g_mix, 0)
            with act.Fori(0, (V0 - QK0) // RING) as r:
                for s in range(RING):
                    act.wait_ge(block_used, r * RING + (s + 1))
                    act.activation(qk_T[:, bass.ds(r * RING + s, 1), :], proj[s % 2][:, 0:T].unsqueeze(1),
                                   ACT.Copy).then_inc(proj_taken, 1)
                    highs(RING, r, s)
            for n in range(V0, CONV0):
                act.wait_ge(block_used, n + 1)
                if n == CONV0 - 1:
                    act.activation(v_sb, acc[:, 0:2, :], ACT.Copy).then_inc(act_step, 1)
                high(n + RING, n % RING)
            for st in range(WOUT0 - CONV0):
                n, c = CONV0 + st, st // 3
                act.wait_ge(block_used, n + 1)
                if st % 3 == 0:
                    if c >= 2:
                        act.wait_ge(conv_taken, 2 * (c - 2) + 1)
                    act.activation(c_gate[:, c % 2, :], proj[n % 2][:, 0:T], ACT.Copy).then_inc(proj_taken, 1)
                if st < HEADS:
                    b = st % 2
                    act.wait_ge(masked_ready, st + 1)
                    if st >= 2:
                        act.wait_ge(turned_ready, st - 1)
                    act.activation(probs[:, b, 0:P], masked[:, b, 0:P], ACT.Exp,
                                   bias=neg_max[:, b, 0:1], accum_out=prob_sum[:, b, 0:1])
                    act.activation(probs[:, b, P:384], masked[:, b, P:384], ACT.Exp,
                                   bias=neg_max[:, b, 1:2], accum_out=prob_sum[:, b, 1:2]
                                   ).then_inc(exp_ready, 1)
                high(n + RING, n % RING)
                if 2 <= st < HEADS + 2:
                    h = st - 2
                    act.wait_ge(turned_ready, h + 1)
                    if h >= 2:
                        act.wait_ge(head_ready, h - 1)
                    act.activation(probs_T[:, h % 2, :], acc[:, 2 + h % 2, 0:384], ACT.Copy
                                   ).then_inc(turned_taken, 1)
                if 3 <= st < HEADS + 3 and st % 2 == 0:
                    h = st - 3
                    act.wait_ge(head_ready, h + 1)
                    act.activation(mixer_T[:, 4 + h // 2, :], acc[:, (h // 2) % 2, 0:T], ACT.Copy)
                    act.activation(mixer_sq[:, 4 + h // 2, :], acc[:, (h // 2) % 2, 0:T], ACT.Square
                                   ).then_inc(heads_taken, 1)
            act.preload_act_table(ACT.Sqrt)
            for c in range(4):
                act.wait_ge(conv_taken, 2 * c + 2)
                act.activation(mixer_sq[:, c, :], mixer_T[:, c, :], ACT.Square).then_inc(conv_squared, 1)
            root(MS_MIXER, rstd_rows, rstd_rows)
            for c in range(KC):
                act.wait_ge(mixed_ready, c + 1)
                act.activation(act_hi[:, c, :], mixed[:, c, :], ACT.Copy).then_inc(act_high, 1)
            with act.Fori(0, (WQ0 - WOUT0) // RING) as r:
                for s in range(RING):
                    act.wait_ge(block_used, r * RING + (WOUT0 + s + 1))
                    highs(WOUT0 + RING, r, s)
            sum_of_squares(x_mixed, 1, [(dve_ready, X_MIXED + t) for t in range(TT)])
            act.dma_start(x_mixed_dram.rearrange("(t p) n -> p t n", p=P), x_mixed).then_inc(x_spilled, 16)
            root(MS_X_MIXED, stats[:, 2:4], ms)
            transposed_high(g_ffn, KC // 2)
            def key_scores_out(q):
                for t in range(TT):
                    act.wait_ge(key_scores, TT * q + t + 1)
                    act.activation(scores[:, t, 4 * q:4 * q + 4, :],
                                   work[t][:, :].rearrange("p (h n) -> p h n", n=NKEYS),
                                   ACT.Copy).then_inc(key_scores_taken, 1)

            for k in range(DOWN0 - WQ0):
                act.wait_ge(block_used, WQ0 + k + 1)
                act.activation(query_T[:, k, :], proj[k % 2][:, 0:T], ACT.Copy).then_inc(proj_taken, 1)
                high(WQ0 + k + RING, k % RING)
                if k >= 6 and k % 4 == 2:
                    key_scores_out((k - 6) // 4)
            key_scores_out(3)
            act.preload_act_table(ACT.Gelu)
            with act.Fori(0, EARLY // RING - 1) as r:
                for s in range(RING):
                    act.wait_ge(block_used, r * RING + (DOWN0 + s + 1))
                    act.activation(experts[:, bass.ds(r * RING + s, 1), :], proj[s % 2][:, 0:T].unsqueeze(1),
                                   ACT.Gelu).then_inc(proj_taken, 1)
                    highs(DOWN0 + RING, r, s)
            for s in range(RING):
                i = EARLY - RING + s
                act.wait_ge(block_used, DOWN0 + i + 1)
                act.activation(experts[:, i, :], proj[s % 2][:, 0:T], ACT.Gelu).then_inc(proj_taken, 1)
                if s < 2:
                    high(HELD0 + s, s)
            act.wait_ge(dve_ready, PICKED_SCORES)
            act.activation(picked[:, 2], picked[:, 2], ACT.Exp).then_inc(act_step, 1)
            act.wait_ge(pe_step, PE_PICKED)
            act.activation(picked_T[:, 0:2, :], work[0][:, :].rearrange("p (a t) -> p a t", t=T), ACT.Copy)
            act.activation(picked_T[:, 2, :], work[1][:, 0:T], ACT.Copy).then_inc(act_step, 1)
            act.wait_ge(x_spilled, 16)
            act.preload_act_table(ACT.Gelu)
            with act.Fori(0, HELD // RING) as r:
                for b in range(RING):
                    act.wait_ge(block_used, r * RING + (HELD0 + b + 1))
                    held = acc[:, bass.ds(r * 2 + b // 2, 1), (b % 2) * T:(b % 2 + 1) * T]
                    act.activation(held, held, ACT.Gelu).then_inc(proj_taken, 1)
                    high(None, (b + 2) % RING, r * 32 + 16 * raw_use(HELD0 + b + 2), b % 2)
                    for g in range(SPAN):
                        at = RING * SPAN * r + (b * SPAN + g)
                        act.wait_ge(router_ready, at + 1)
                        act.activation(experts[:, EARLY:NKEYS, bass.ds(at * QUAD, QUAD)]
                                       .rearrange("p i u -> p u i"),
                                       routed[g % RING].rearrange("p (u i) -> p u i", i=NKEYS)[:, :, EARLY:NKEYS],
                                       ACT.Copy).then_inc(router_act, 1)

            def weight_high(m, b, ready):
                act.wait_ge(w_ready, ready)
                act.activation(w_hi[:, b, :].unsqueeze(1), experts[:, m, :], ACT.Copy).then_inc(w_hi_ready, 1)

            for b in range(2):
                weight_high(slice(b, b + 1), b, b + 1)
            for s in (2, 3):
                high(PAIR0 + s, s)
            with act.Fori(0, PAIRS // 2) as r:
                for b in range(2):
                    act.wait_ge(block_used, r * 4 + (PAIR0 + 2 * b + 1))
                    act.wait_ge(w_ready, r * 2 + (AHEAD + b - 1))
                    act.activation(gelu_ring[:, b, :], proj[b][:, 0:T], ACT.Gelu).then_inc(proj_taken, 1)
                    highs(PAIR0 + RING, r, 2 * b)
                    act.wait_ge(block_used, r * 4 + (PAIR0 + 2 * b + 2))
                    weight_high(bass.ds(r * 2 + (b + 2), 1), b, r * 2 + (b + 3))
                    highs(PAIR0 + RING, r, 2 * b + 1)
            with act.Fori(0, AHEAD // RING - 1) as r:
                for s in range(RING):
                    act.wait_ge(block_used, r * RING + (UP0 + s + 1))
                    weight_high(bass.ds(r * RING + (PAIRS + s + 2), 1), s % 2, r * RING + (PAIRS + s + 3))
                    highs(UP0 + RING, r, s)
            for s in range(2):
                m = NKEYS - 2 + s
                act.wait_ge(block_used, BLOCKS - RING + s + 1)
                weight_high(slice(m, m + 1), s, m + 1)
            act.preload_act_table(ACT.Sqrt)
            for t in range(TT):
                act.wait_ge(total_ready, t + 1)
                act.activation(final_sq[t], acc[:, 2 * t:2 * t + 2, :].rearrange("p a n -> p (a n)"),
                               ACT.Square, accum_out=sumsq[:, 2, t:t + 1]).then_inc(final_sum, 1)
            for t in range(TT):
                act.wait_ge(final_ms, t + 1)
                act.activation(stats[:, 2 + t:3 + t], ms[:, t:t + 1], ACT.Sqrt).then_inc(final_root, 1)

        @block.vector
        def _(dve):
            chain = [0]

            def link(done):
                chain[0] += 1
                done.then_inc(dve_step, 1)
                dve.wait_ge(dve_step, chain[0])

            def low(n, s):
                dve.wait_ge(hi_ready, n + 1)
                dve.tensor_tensor(lo[:, s, :], raw[:, s, :], hi[:, s, :].bitcast(f32),
                                  ALU.subtract).then_inc(lo_by_dve, 1)

            def scaled(source, step):
                dve.wait_ge(act_step, step)
                link(dve.reciprocal(rstd, stats[:, 2:4]))
                for t in range(TT):
                    done = dve.tensor_scalar(x_scaled[:, t, :], source[:, t, :], rstd[:, t:t + 1], None, ALU.mult)
                link(done)

            def transposed_low(gains, first):
                for k in range(KC):
                    dve.wait_ge(act_high, first + k // 2 + 1)
                    done = dve.scalar_tensor_tensor(act_lo[:, k, :], acc_view(k), gains[:, k:k + 1],
                                                    act_hi[:, k, :].bitcast(f32), ALU.mult, ALU.subtract)
                    if k % 2:
                        done.then_inc(act_split, 1)

            dve.wait_ge(act_step, ACT_SUMSQ1)
            dve.tensor_scalar(ms, sumsq[:, 0, :], 1.0 / D, EPS, ALU.mult, ALU.add).then_inc(dve_ready, 1)
            scaled(x_sb, ACT_ROOT1)
            assert chain[0] == DVE_SCALED, chain[0]
            dve.memset(padded[:, :, 0:2], 0.0)
            low(1, 1)
            low(3, 3)
            transposed_low(g_mix, SPLIT_X)
            for n in range(5, CONV0, 2):
                low(n, n % RING)
            for st in range(WOUT0 - CONV0 + 1):
                n, c = CONV0 + st, st // 3
                if 1 <= st <= HEADS:
                    h = st - 1
                    b = h % 2
                    dve.wait_ge(exp_ready, h + 1)
                    link(dve.reciprocal(prob_inv[:, b, :], prob_sum[:, b, :]))
                    dve.tensor_scalar(probs[:, b, 0:P], probs[:, b, 0:P], prob_inv[:, b, 0:1], None, ALU.mult)
                    dve.tensor_scalar(probs[:, b, P:384], probs[:, b, P:384], prob_inv[:, b, 1:2], None,
                                      ALU.mult).then_inc(probs_ready, 1)
                if st == WOUT0 - CONV0:
                    break
                if st % 3 == 1:
                    dve.wait_ge(proj_taken, 8 + c + 1)
                    dve.wait_ge(block_used, n + 1)
                    b = c % 2
                    done = dve.tensor_tensor(padded[:, b, 2:T + 2], proj[n % 2][:, 0:T], c_gate[:, b, :], ALU.mult)
                    done.then_inc(conv_taken, 1)
                    dve.wait_ge(conv_taken, 2 * c + 1)
                    link(dve.tensor_scalar(taps[:, b, 0, :], padded[:, b, 2:T + 2], conv_w[:, c, 2:3], None, ALU.mult))
                    link(dve.scalar_tensor_tensor(taps[:, b, 1, :], padded[:, b, 1:T + 1], conv_w[:, c, 1:2],
                                                  taps[:, b, 0, :], ALU.mult, ALU.add))
                    link(dve.scalar_tensor_tensor(taps[:, b, 2, :], padded[:, b, 0:T], conv_w[:, c, 0:1],
                                                  taps[:, b, 1, :], ALU.mult, ALU.add))
                if st % 3 == 2:
                    dve.wait_ge(block_used, n + 1)
                    dve.tensor_tensor(mixer_T[:, c, :], proj[n % 2][:, 0:T], taps[:, c % 2, 2, :],
                                      ALU.mult).then_inc(conv_taken, 1)
                if st < HEADS:
                    b = st % 2
                    dve.wait_ge(scores_ready, st + 1)
                    if st >= 2:
                        dve.wait_ge(exp_ready, st - 1)
                    link(dve.scalar_tensor_tensor(masked[:, b, :], work[b][:, 0:384], float(HD) ** -0.5,
                                                  mask, ALU.mult, ALU.add))
                    dve.reduce_max(neg_max[:, b, 0:1], masked[:, b, 0:P], AX.X, negate=True)
                    dve.reduce_max(neg_max[:, b, 1:2], masked[:, b, P:384], AX.X, negate=True
                                   ).then_inc(masked_ready, 1)
                if n + RING >= WOUT0 and n % 2:
                    low(n + RING, n % RING)
            dve.wait_ge(pe_step, PE_NORMS)
            link(dve.tensor_scalar(rstd_rows[:, 0, :], work[0][:, 0:T], 1.0 / 512, EPS, ALU.mult, ALU.add))
            dve.tensor_scalar(rstd_rows[:, 1, :], work[1][:, 0:T], 1.0 / 512, EPS, ALU.mult,
                              ALU.add).then_inc(dve_ready, 1)
            dve.wait_ge(act_step, ACT_ROOT2)
            link(dve.reciprocal(rstd_rows, rstd_rows))
            for c in range(KC + 2):
                if c < KC:
                    dve.scalar_tensor_tensor(mixed[:, c, :], mixer_T[:, c, :], g_out[:, c:c + 1],
                                             rstd_rows[:, c // 4, :], ALU.mult, ALU.mult).then_inc(mixed_ready, 1)
                if c >= 2:
                    dve.wait_ge(act_high, SPLIT_MIXER + c - 1)
                    dve.tensor_tensor(act_lo[:, c - 2, :], mixed[:, c - 2, :], act_hi[:, c - 2, :].bitcast(f32),
                                      ALU.subtract).then_inc(act_split, 1)
            for n in range(WOUT0 + RING + 1, WQ0 + RING, 2):
                low(n, n % RING)
            dve.wait_ge(block_used, WQ0)
            for t in range(TT):
                dve.tensor_tensor(x_mixed[:, t, :].rearrange("p (a n) -> p a n", a=2),
                                  acc[:, 2 * t:2 * t + 2, :],
                                  x_sb[:, t, :].rearrange("p (a n) -> p a n", a=2), ALU.add).then_inc(dve_ready, 1)
            dve.wait_ge(act_step, ACT_SUMSQ3)
            dve.tensor_scalar(ms, sumsq[:, 1, :], 1.0 / D, EPS, ALU.mult, ALU.add).then_inc(dve_ready, 1)
            scaled(x_mixed, ACT_ROOT3)
            assert chain[0] == DVE_SCALED2, chain[0]
            transposed_low(g_ffn, SPLIT_X_MIXED)

            taken = [0]

            def step(done):
                taken[0] += 1
                done.then_inc(topk_step, 1)
                return taken[0]

            def top16(values, left, best, at, rows):
                first = [step(dve.max(best[:, h, 0:8], values[:, h, :])) for h in range(rows)]
                for h in range(rows):
                    dve.wait_ge(topk_step, first[h])
                    step(dve.max_index(at[:, h, 0:8], best[:, h, 0:8], values[:, h, :]))
                rest = []
                for h in range(rows):
                    rest.append(step(dve.match_replace(left[:, h, :], best[:, h, 0:8], values[:, h, :], LOWEST)))
                second = []
                for h in range(rows):
                    dve.wait_ge(topk_step, rest[h])
                    second.append(step(dve.max(best[:, h, 8:16], left[:, h, :])))
                for h in range(rows):
                    dve.wait_ge(topk_step, second[h])
                    last = step(dve.max_index(at[:, h, 8:16], best[:, h, 8:16], left[:, h, :]))
                dve.wait_ge(topk_step, last)

            for q in range(4):
                for t in range(TT):
                    rows = slice(4 * q, 4 * q + 4)
                    dve.wait_ge(key_scores_taken, TT * q + t + 1)
                    top16(scores[:, t, rows, :], scores_left, top1[:, t, rows, :], top1_at[:, t, rows, :], 4)
            for t in range(TT):
                link(dve.tensor_copy(first_index, top1_at[:, t]))
                halves = top1[:, t].rearrange("p (h a) k -> p h a k", a=2)
                link(dve.tensor_tensor(
                    pairs.rearrange("p h (a b) -> p h a b", b=TOPK),
                    halves[:, :, 0, :].unsqueeze(3).to_broadcast([P, PH, TOPK, TOPK]),
                    halves[:, :, 1, :].unsqueeze(2).to_broadcast([P, PH, TOPK, TOPK]), ALU.add))
                best = picked[:, 2, t, :].rearrange("p (h k) -> p h k", k=TOPK)
                top16(pairs, pairs_left, best, pos.rearrange("p (h k) -> p h k", k=TOPK), PH)
                dve.tensor_scalar(pos_ab[:, 0, :], pos, 4, None, ALU.logical_shift_right)
                link(dve.tensor_scalar(pos_ab[:, 1, :], pos, 15, None, ALU.bitwise_and))
                link(dve.tensor_copy(ranks, pos_ab))
                for a in range(2):
                    link(dve.tensor_tensor(lookup,
                                           iota[:, 0:TOPK].unsqueeze(1).to_broadcast([P, PH * TOPK, TOPK]),
                                           ranks[:, a, :].unsqueeze(2).to_broadcast([P, PH * TOPK, TOPK]),
                                           ALU.is_equal))
                    spread = lookup.rearrange("p (h k) a -> p h k a", k=TOPK)
                    number = first_index.rearrange("p (h a) k -> p h a k", a=2)[:, :, a, :]
                    link(dve.tensor_tensor(spread, spread,
                                           number.unsqueeze(2).to_broadcast([P, PH, TOPK, TOPK]), ALU.mult))
                    link(dve.reduce_sum(picked[:, a, t, :], lookup, AX.X))
                peak = stats[:, 40:48]
                link(dve.tensor_copy(peak, best[:, :, 0]))
                link(dve.tensor_tensor(best, best, peak.unsqueeze(2).to_broadcast([P, PH, TOPK]), ALU.subtract))
            dve.memset(gate_sum, 0.0).then_inc(dve_ready, 1)
            dve.wait_ge(dve_ready, PICKED_SCORES)
            dve.wait_ge(act_step, ACT_EXP)
            gates = picked[:, 2].rearrange("p t (h k) -> p (t h) k", k=TOPK)
            link(dve.reduce_sum(gate_sum, gates, AX.X))
            link(dve.reciprocal(gate_sum, gate_sum))
            link(dve.tensor_tensor(gates, gates, gate_sum.unsqueeze(2).to_broadcast([P, TT * PH, TOPK]), ALU.mult))
            assert chain[0] == DVE_PICKED, chain[0]

            def hots(g, s):
                def token(c):
                    return (picked_T[:, c, bass.ds(g * QUAD, QUAD)].unsqueeze(2)
                            .to_broadcast([P, QUAD, NKEYS]))
                numbers = iota[:, :].unsqueeze(1).to_broadcast([P, QUAD, NKEYS])
                dve.tensor_tensor(hot_j[s], numbers, token(1), ALU.is_equal)
                dve.tensor_tensor(hot_i[:, s], numbers, token(0), ALU.is_equal).then_inc(hot_ready, 1)

            def rows_in_place(g, s):
                dve.wait_ge(router_act, g + 1)
                rows = experts[:, 0:EARLY, bass.ds(g * QUAD, QUAD)].rearrange("p i u -> p u i")
                return dve.tensor_tensor(rows, routed[s].rearrange("p (u i) -> p u i", i=NKEYS)[:, :, 0:EARLY],
                                         rows, ALU.mult)

            dve.wait_ge(act_step, ACT_PICKED)
            dve.wait_ge(lo_by_pool, pool_splits(HELD0 - 1))
            for s in range(RING):
                hots(s, s)
            with dve.Fori(0, GROUPS // RING - 1) as r:
                for s in range(RING):
                    rows_in_place(r * RING + s, s)
                    hots(r * RING + (RING + s), s)
            for s in range(RING - 1):
                rows_in_place(GROUPS - RING + s, s)
            rows_in_place(GROUPS - 1, RING - 1).then_inc(w_ready, EARLY)

            def weight_low(m, b, ready):
                dve.wait_ge(w_hi_ready, ready)
                dve.tensor_tensor(w_lo[:, b, :].unsqueeze(1), experts[:, m, :],
                                  w_hi[:, b, :].bitcast(f32).unsqueeze(1), ALU.subtract).then_inc(w_lo_ready, 1)

            dve.wait_ge(proj_taken, 28 + AHEAD)
            for h in range(HELD):
                row = experts[:, EARLY + h, :]
                dve.tensor_tensor(row, acc_view(h), row, ALU.mult).then_inc(w_ready, 1)
            low(PAIR0 + 1, 1)
            for b in range(2):
                weight_low(slice(b, b + 1), b, b + 1)
            low(PAIR0 + 3, 3)
            with dve.Fori(0, PAIRS // 2) as r:
                for b in range(2):
                    dve.wait_ge(proj_taken, r * 2 + (28 + AHEAD + b + 1))
                    row = experts[:, bass.ds(r * 2 + (AHEAD + b), 1), :]
                    dve.tensor_tensor(row, row, gelu_ring[:, b, :].unsqueeze(1), ALU.mult).then_inc(w_ready, 1)
                    weight_low(bass.ds(r * 2 + (b + 2), 1), b, r * 2 + (b + 3))
                    low(r * RING + (PAIR0 + RING + 2 * b + 1), 2 * b + 1)
            with dve.Fori(0, AHEAD // RING - 1) as r:
                for s in range(RING):
                    weight_low(bass.ds(r * RING + (PAIRS + s + 2), 1), s % 2, r * RING + (PAIRS + s + 3))
                    low(r * RING + (UP0 + RING + s), s)
            for s in range(2):
                m = NKEYS - 2 + s
                weight_low(slice(m, m + 1), s, m + 1)

            dve.wait_ge(gain_loaded, 16)
            for t in range(TT):
                dve.wait_ge(final_sum, t + 1)
                dve.tensor_scalar(ms[:, t:t + 1], sumsq[:, 2, t:t + 1], 1.0 / D, EPS, ALU.mult,
                                  ALU.add).then_inc(final_ms, 1)
            for t in range(TT):
                dve.wait_ge(final_root, t + 1)
                link(dve.reciprocal(rstd[:, t:t + 1], stats[:, 2 + t:3 + t]))
                dve.scalar_tensor_tensor(result[:, t, :], acc[:, 2 * t:2 * t + 2, :].rearrange("p a n -> p (a n)"),
                                         rstd[:, t:t + 1], final_gain, ALU.mult, ALU.mult).then_inc(result_ready, 1)

        @block.tensor
        def _(pe):
            def rows_product(s, target, split=None):
                for k in range(KC):
                    if split is not None and k % 2 == 0:
                        pe.wait_ge(act_split, split + k // 2 + 1)
                    part = slice(k * P, (k + 1) * P)
                    pe.matmul(target, hi[:, s, part], act_hi[:, k, :], start=(k == 0), stop=False)
                    pe.matmul(target, hi[:, s, part], act_lo[:, k, :], start=False, stop=False)
                    done = pe.matmul(target, lo[:, s, part], act_hi[:, k, :], start=False, stop=(k == KC - 1))
                return done

            def token_product(left_hi, left_lo, right, target, width, start, stop, tiles=range(TT)):
                for t in tiles:
                    part = slice(t * P, (t + 1) * P)
                    for left, rights in ((left_hi, (hi, lo)), (left_lo, (hi,))):
                        for r in rights:
                            for half in range(width):
                                done = pe.matmul(target(t, half), left[:, part], right(r, half),
                                                 start=start and left is left_hi and r is hi,
                                                 stop=stop and left is left_lo)
                return done

            def transposes(seen):
                pe.wait_ge(dve_step, seen)
                for k in range(KC):
                    for t in range(TT):
                        done = pe.transpose(acc_view(k)[:, t * P:(t + 1) * P],
                                            x_scaled[:, t, k * P:(k + 1) * P], ident[:, :])
                    if k % 2:
                        done.then_inc(turned, 1)

            pe.wait_ge(consts_loaded, 64)
            transposes(DVE_SCALED)
            for n in range(QK0, V0):
                wait_low(pe, n)
                if n >= 2:
                    pe.wait_ge(proj_taken, n - 1)
                rows_product(n % RING, proj[n % 2][:, 0:T], SPLIT_X if n == 0 else None).then_inc(block_used, 1)
            for n in range(V0, CONV0):
                wait_low(pe, n)
                s = n % RING
                for c in range(2):
                    k = 2 * (n - V0) + c
                    done = token_product(act_hi[:, k, :], act_lo[:, k, :],
                                         lambda r, half: r[:, s, c * 512:(c + 1) * 512],
                                         lambda t, half: acc[:, t, :], 1, k == 0, k == KC - 1)
                done.then_inc(block_used, 1)
            for st in range(WOUT0 - CONV0):
                n, c = CONV0 + st, st // 3
                wait_low(pe, n)
                if st >= 2:
                    before = st - 2
                    if before % 3 == 0:
                        pe.wait_ge(proj_taken, 8 + before // 3 + 1)
                    else:
                        pe.wait_ge(conv_taken, 2 * (before // 3) + before % 3)
                else:
                    pe.wait_ge(proj_taken, 8)
                rows_product(n % RING, proj[n % 2][:, 0:T]).then_inc(block_used, 1)
                if st < HEADS:
                    if st >= 2:
                        pe.wait_ge(masked_ready, st - 1)
                    rows = slice(HD * (st % 2), HD * (st % 2) + HD)
                    q, k = qk_T[rows, st // 2, :], qk_T[rows, 4 + st // 2, :]
                    pe.matmul(work[st % 2][:, 0:P], q[:, 0:P], k[:, 0:P], start=True, stop=True)
                    pe.matmul(work[st % 2][:, P:384], q[:, P:T], k, start=True, stop=True
                              ).then_inc(scores_ready, 1)
                if 2 <= st < HEADS + 2:
                    h = st - 2
                    pe.wait_ge(probs_ready, h + 1)
                    if h >= 2:
                        pe.wait_ge(turned_taken, h - 1)
                    for b in range(3):
                        done = pe.transpose(acc[:, 2 + h % 2, b * P:(b + 1) * P],
                                            probs[:, h % 2, b * P:(b + 1) * P], ident[:, :])
                    done.then_inc(turned_ready, 1)
                if 3 <= st < HEADS + 3:
                    h = st - 3
                    pe.wait_ge(turned_taken, h + 1)
                    if h == 0:
                        pe.wait_ge(act_step, ACT_V)
                    if h >= 4 and h % 2 == 0:
                        pe.wait_ge(heads_taken, h // 2 - 1)
                    rows = slice(HD * (h % 2), HD * (h % 2) + HD)
                    target = acc[rows, (h // 2) % 2, :]
                    vh = v_sb[:, :, h * HD:(h + 1) * HD]
                    pe.matmul(target[:, 0:P], vh[:, 0, :], probs_T[:, h % 2, 0:P], start=True, stop=True)
                    pe.matmul(target[:, P:T], vh[:, 0, :], probs_T[:, h % 2, P:2 * P], start=True, stop=False)
                    pe.matmul(target[:, P:T], vh[:, 1, :], probs_T[:, h % 2, 2 * P:384], start=False,
                              stop=True).then_inc(head_ready, 1)
            for half in (1, 0):
                for c in range(4):
                    if half:
                        pe.wait_ge(heads_taken, c + 1)
                    else:
                        pe.wait_ge(conv_squared, c + 1)
                    done = pe.matmul(work[half][:, 0:T], ones, mixer_sq[:, 4 * half + c, :],
                                     start=(c == 0), stop=(c == 3))
            done.then_inc(pe_step, 1)
            for n in range(WOUT0, WQ0):
                wait_low(pe, n)
                s, c = n % RING, n - WOUT0
                pe.wait_ge(act_split, SPLIT_MIXER + c + 1)
                token_product(act_hi[:, c, :], act_lo[:, c, :],
                              lambda r, half: r[:, s, half * 512:(half + 1) * 512],
                              lambda t, half: acc[:, 2 * t + half, :], 2, c == 0, c == KC - 1
                              ).then_inc(block_used, 1)
            transposes(DVE_SCALED2)

            def key_products(q):
                pe.wait_ge(proj_taken, 12 + 4 * q + 4)
                for t in range(TT):
                    if q:
                        pe.wait_ge(key_scores_taken, TT * (q - 1) + t + 1)
                    for h in range(4):
                        row = 4 * q + h
                        done = pe.matmul(work[t][:, h * NKEYS:(h + 1) * NKEYS],
                                         query_T[:, row, t * P:(t + 1) * P], keys_sb[:, row, :],
                                         start=True, stop=True)
                    done.then_inc(key_scores, 1)

            pe.wait_ge(keys_loaded, 16)
            for k in range(DOWN0 - WQ0):
                wait_low(pe, WQ0 + k)
                pe.wait_ge(proj_taken, 12 + k - 1)
                rows_product(k % RING, proj[k % 2][:, 0:T], SPLIT_X_MIXED if k == 0 else None
                             ).then_inc(block_used, 1)
                if k >= 5 and k % 4 == 1:
                    key_products((k - 5) // 4)
            key_products(3)
            with pe.Fori(0, EARLY // RING) as r:
                for s in range(RING):
                    pe.wait_ge(lo_by_pool, r * RING + pool_splits(DOWN0 + s))
                    pe.wait_ge(proj_taken, r * RING + (28 + s - 1))
                    rows_product(s, proj[s % 2][:, 0:T]).then_inc(block_used, 1)
            pe.wait_ge(dve_step, DVE_PICKED)
            for c in range(3):
                for t in range(TT):
                    at = (2 * c + t) % 4
                    done = pe.transpose(work[c // 2][:, at * P:(at + 1) * P], picked[:, c, t, :], ident[:, :])
            done.then_inc(pe_step, 1)

            with pe.Fori(0, HELD // RING) as r:
                for b in range(RING):
                    pe.wait_ge(lo_by_pool, r * RING + pool_splits(HELD0 + b))
                    pe.wait_ge(proj_taken, r * RING + (28 + EARLY + b))
                    rows_product(b, acc[:, bass.ds(r * 2 + b // 2, 1), (b % 2) * T:(b % 2 + 1) * T]
                                 ).then_inc(block_used, 1)
                    for g in range(SPAN):
                        s = g % RING
                        pe.wait_ge(hot_weighted, RING * SPAN * r + (b * SPAN + g + 1))
                        for u in range(QUAD):
                            one_j = hot_j[s][:, u, :]
                            done = pe.matmul(routed[s][:, u * NKEYS:(u + 1) * NKEYS],
                                             one_j.bitcast(f32) if s < 2 else one_j, hot_i[:, s, u, :],
                                             start=True, stop=True)
                        done.then_inc(router_ready, 1)

            def up(s, b, stop=False, tiles=range(TT), start=False):
                return token_product(w_hi[:, b, :], w_lo[:, b, :],
                                     lambda r, half: r[:, s, half * 512:(half + 1) * 512],
                                     lambda t, half: acc[:, 2 * t + half, :], 2, start, stop, tiles)

            pe.wait_ge(w_ready, EARLY)

            def pair(r, b, first=False):
                pe.wait_ge(lo_by_pool, r * 2 + pool_splits(PAIR0 + 2 * b))
                pe.wait_ge(proj_taken, r * 2 + (28 + AHEAD + b - 1))
                rows_product(2 * b, proj[b][:, 0:T]).then_inc(block_used, 1)
                pe.wait_ge(lo_by_dve, r * 2 + dve_splits(PAIR0 + 2 * b + 1))
                pe.wait_ge(w_lo_ready, r * 2 + (b + 1))
                if first:
                    pe.wait_ge(w_ready, AHEAD)
                up(2 * b + 1, b, start=first).then_inc(block_used, 1)

            pair(0, 0, True)
            pair(0, 1)
            with pe.Fori(1, PAIRS // 2) as r:
                for b in range(2):
                    pair(r, b)
            for s in range(RING):
                wait_low(pe, UP0 + s)
                pe.wait_ge(w_lo_ready, PAIRS + s + 1)
                up(s, s % 2).then_inc(block_used, 1)
            with pe.Fori(0, AHEAD // RING - 2) as r:
                for s in range(RING):
                    pe.wait_ge(lo_by_dve, r * RING + dve_splits(MIXED_LO + s))
                    pe.wait_ge(w_lo_ready, r * RING + (PAIRS + RING + s + 1))
                    up(s, s % 2).then_inc(block_used, 1)
            pe.wait_ge(x_reloaded, 16)
            for t in range(TT):
                for half in range(2):
                    pe.matmul(acc[:, 2 * t + half, :], ident[:, :], x_again[:, t, half * 512:(half + 1) * 512],
                              start=False, stop=False)
            for s in range(RING):
                wait_low(pe, BLOCKS - RING + s)
                pe.wait_ge(w_lo_ready, NKEYS - RING + s + 1)
                if s < RING - 1:
                    up(s, s % 2).then_inc(block_used, 1)
                else:
                    for t in range(TT):
                        up(s, s % 2, True, [t]).then_inc(total_ready, 1)


def columns_of(w, first, count):
    part = w[:, first:first + count * P].reshape(KC, P, count, P)
    return part.transpose(2, 1, 0, 3).reshape(count, P, D)


def kernel(x, norm_mix_g, w_in, conv_w, norm_conv_out_g, norm_attn_out_g, w_out, norm_ffn_g, peer_w_query,
           peer_sub_keys1, peer_sub_keys2, peer_down, peer_up, final_norm_g):
    import numpy as np
    import concourse.bacc as bacc
    from concourse.bass_utils import run_bass_kernel_spmd

    w_in, w_out, wq = np.asarray(w_in)[0], np.asarray(w_out)[0], np.asarray(peer_w_query)[0]
    down, up = np.asarray(peer_down)[0], np.asarray(peer_up)[0]
    b_cols, c_cols, h_cols = (columns_of(w_in, 512 * g, 4) for g in range(3))
    down = down.reshape(NKEYS, NKEYS, KC, P).transpose(0, 3, 2, 1).reshape(NKEYS, P, D)
    up = up.reshape(NKEYS, NKEYS, D)
    parts = [
        columns_of(w_in, 1536, 8),
        w_in[:, 2560:3072].reshape(4, 2, P, 512).transpose(0, 2, 1, 3).reshape(4, P, D),
        np.stack([g[c] for c in range(4) for g in (c_cols, h_cols, b_cols)]),
        w_out.reshape(KC, P, D),
        columns_of(wq, 0, 16),
        down[:AHEAD],
        np.stack([down[AHEAD:], up[:PAIRS]], axis=1).reshape(2 * PAIRS, P, D),
        up[PAIRS:],
    ]
    stream = np.concatenate(parts)
    keys = np.stack([np.asarray(peer_sub_keys1)[0], np.asarray(peer_sub_keys2)[0]], axis=1)
    keys = np.ascontiguousarray(keys.transpose(3, 0, 1, 2).reshape(P, 2 * PH * NKEYS))

    def column(g):
        return np.asarray(g).reshape(-1, P).T

    taps = np.asarray(conv_w)[0].reshape(3, 4, P).transpose(2, 1, 0).reshape(P, 12)
    columns = np.ascontiguousarray(np.concatenate(
        [column(norm_mix_g[0]), column(norm_conv_out_g[0]), column(norm_attn_out_g[0]), column(norm_ffn_g[0]), taps],
        axis=1))
    n = np.arange(P)
    future = np.where(n[None, :] > n[:, None], NEG, 0.0)
    consts = np.concatenate([np.eye(P), np.tile(n, (P, 1)), future, np.zeros((P, P)), future, np.ones((P, P))],
                            axis=1).astype(np.float32)
    arrays = {
        "x": np.ascontiguousarray(np.asarray(x)[0]), "stream": stream, "keys": keys, "columns": columns,
        "consts": consts, "final_g": np.asarray(final_norm_g),
    }
    nc = bacc.Bacc("TRN2", target_bir_lowering=False, num_devices=1)
    args = [nc.dram_tensor(f"in_{k}", a.shape, mybir.dt.from_np(a.dtype), kind="ExternalInput").ap()
            for k, a in arrays.items()]
    args.append(nc.dram_tensor("x_mixed_dram", (T, D), mybir.dt.float32, kind="Internal").ap())
    args.append(nc.dram_tensor("out_x", (T, D), mybir.dt.float32, kind="ExternalOutput").ap())
    block_kernel(nc, *args)
    r = run_bass_kernel_spmd(nc, [{f"in_{k}": a for k, a in arrays.items()}], core_ids=[0])
    return r.results[0]["out_x"].reshape(1, T, D)
```

```python
import concourse.bass as bass
from concourse import mybir
from contextlib import ExitStack

P = 128
T = 256
TT = T // P
D = 1024
KC = D // P
HEADS, HD = 8, 64
NKEYS = 128
PH, TOPK = 8, 16
EPS = 1e-6
NEG = -1e30
LOWEST = -3.4e38

QK0, V0, CONV0, WOUT0, WQ0, DOWN0 = 0, 8, 12, 24, 32, 48
EARLY = 32
HELD = 8
AHEAD = EARLY + HELD
HELD0 = DOWN0 + EARLY
PAIR0 = DOWN0 + AHEAD
PAIRS = NKEYS - AHEAD
UP0 = PAIR0 + 2 * PAIRS
BLOCKS = UP0 + AHEAD
RING = 4
POOL0 = WQ0 + RING
MIXED_LO = UP0 + RING
QUAD = 4
GROUPS = T // QUAD
SPAN = GROUPS // HELD
BY_POOL = QUAD - 2
HIGH_AT = (2, 4)
LOW_AT = (6, 7)
LOOK = 2
OUT_PIECES = [[(0, 2)], [(0, 1), (1, 2)]]

(ACT_V, ACT_ROOT_MIXER, ACT_EXP, ACT_PICKED) = range(1, 5)
(X_MIXED, X_MIXED_B, PICKED_SCORES) = range(1, 4)
NORM_X, NORM_X_MIXED, NORM_FINAL = range(3)
SPLIT_X, SPLIT_MIXER, SPLIT_X_MIXED = 0, 4, 12
PE_NORMS, PE_PICKED = range(1, 3)
DVE_PICKED = 62


def split_by_pool(n):
    if CONV0 <= n < WOUT0 or POOL0 <= n < PAIR0:
        return True
    return n < MIXED_LO and n % 2 == 0


POOL_SPLITS = [sum(split_by_pool(m) for m in range(n + 1)) for n in range(BLOCKS)]


def pool_splits(n):
    return POOL_SPLITS[n]


def raw_use(n):
    if n < HELD0:
        return n // RING + 1
    if n < PAIR0:
        return HELD0 // RING + (n - HELD0) // 2 + 1
    return HELD0 // RING + (HELD // 2 if n % RING < 2 else 0) + (n - PAIR0) // RING + 1


def dve_splits(n):
    return n + 1 - POOL_SPLITS[n]


def block_kernel(nc, x, stream, keys, columns, consts, final_g, x_mixed_dram, out):
    f32, f32r, u32, bf16 = mybir.dt.float32, mybir.dt.float32r, mybir.dt.uint32, mybir.dt.bfloat16
    ALU, ACT, AX = mybir.AluOpType, mybir.ActivationFunctionType, mybir.AxisListType
    ctx = ExitStack()
    with ctx:
        def sb(name, shape, dt=f32):
            return ctx.enter_context(nc.sbuf_tensor(name, shape, dt))

        def sem(name):
            return ctx.enter_context(nc.semaphore(name))

        big = sb("big", [P, NKEYS * T])
        experts = big[:, :].rearrange("p (i t) -> p i t", t=T)
        raw = sb("raw", [P, RING, D])
        hi = sb("hi", [P, RING, D], f32r)
        lo = sb("lo", [P, RING, D], f32r)
        act_hi = sb("act_hi", [P, KC, T], f32r)
        act_lo = sb("act_lo", [P, KC, T], f32r)
        gelu_ring = sb("gelu_ring", [P, 2, T])
        w_hi = sb("w_hi", [P, 2, T], f32r)
        w_lo = sb("w_lo", [P, 2, T], f32r)
        picked_T = sb("picked_T", [P, 2, T])
        picked_i = sb("picked_i", [P, T], bf16)
        iota_quad = sb("iota_quad", [P, NKEYS, QUAD], bf16)
        hot_i = sb("hot_i", [P, RING, NKEYS, QUAD], bf16)
        ident = sb("ident", [P, P])
        ident_r = sb("ident_r", [P, P], f32r)
        iota = sb("iota", [P, P])
        cols = sb("cols", [P, 36])
        stats = sb("stats", [P, 60])

        def view(at, *shape):
            n = 1
            for s in shape:
                n *= s
            v = big[:, at:at + n]
            if len(shape) == 2:
                v = v.rearrange("p (a b) -> p a b", b=shape[1])
            if len(shape) == 3:
                v = v.rearrange("p (a b c) -> p a b c", b=shape[1], c=shape[2])
            return v

        qk_T = view(0, 8, T)
        v_sb = view(2048, TT, 512)
        mixer_T = view(3072, KC, T)
        masked = view(7168, 2, 384)
        probs = view(7936, 2, 384)
        probs_T = view(8704, 2, 384)
        consts_front = view(9472, 512)
        mask, ones = consts_front[:, 0:384], consts_front[:, 384:512]
        small = view(10240, 2048)
        query_T = view(12288, 16, T)
        c_gate = view(12288, 2, T)
        padded = view(12800, 2, T + 2)
        taps = view(13400, 2, 3, T)
        keys_sb = view(16384, 16, NKEYS)
        scores = view(18432, TT, 16, NKEYS)
        scores_left = view(22528, 4, NKEYS)
        first_index = view(23040, 16, TOPK)
        pos_ab = view(23296, 2, P).bitcast(u32)
        ranks = view(23552, 2, P)
        pairs = view(24576, PH, TOPK * TOPK)
        pairs_left = view(26624, PH, TOPK * TOPK)
        x_scaled = view(26624, TT, D)
        square_x = view(24576, TT, D)
        x_mixed = view(28672, TT, D)
        x_sb = view(30720, TT, D)
        lookup = view(30720, PH * TOPK, TOPK)
        mixer_sq = view(18432, KC, T)
        square_sums = view(20480, 2, T)
        top1 = small[:, 0:512].rearrange("p (t h k) -> p t h k", t=TT, k=TOPK)
        top1_at = small[:, 512:1024].bitcast(u32).rearrange("p (t h k) -> p t h k", t=TT, k=TOPK)
        pos = small[:, 1024:1152].bitcast(u32)
        picked = small[:, 1152:1920].rearrange("p (c t k) -> p c t k", c=3, t=TT)
        final_gain = view(0, D)
        result = view(D, TT, D)
        final_sq = [view(3 * D, D), view(4 * D, D)]
        x_again = view(20 * T, TT, D)
        again_hi = act_hi[:, :, :].rearrange("p (t k) c -> p t (k c)", t=TT)
        again_lo = act_lo[:, :, :].rearrange("p (t k) c -> p t (k c)", t=TT)
        hot_w = raw[:, 2:4, :].rearrange("p a (b u n) -> p (a b) u n", b=2, u=QUAD)
        hot_j = [w.rearrange("p a (u n) -> p (a u) n", n=NKEYS) for w in (w_hi[:, :, :], w_lo[:, :, :])]
        hot_j += [hi[:, 2, b * QUAD * NKEYS:(b + 1) * QUAD * NKEYS].rearrange("p (u n) -> p u n", n=NKEYS)
                  for b in range(2)]

        root, rstd, eps = stats[:, 2:4], stats[:, 4:6], stats[:, 48:49]
        root_mixer, rstd_mixer = stats[:, 50:54], stats[:, 54:58]
        sumsq = stats[:, 6:12].rearrange("p (a t) -> p a t", t=TT)
        neg_max = stats[:, 12:16].rearrange("p (a t) -> p a t", t=2)
        prob_sum = stats[:, 16:20].rearrange("p (a t) -> p a t", t=2)
        prob_inv = stats[:, 20:24].rearrange("p (a t) -> p a t", t=2)
        gate_sum = stats[:, 24:40]
        scales = stats[:, 6:6 + 2 * SPAN * (QUAD - BY_POOL)].rearrange("p (a g u) -> p a g u", g=SPAN, u=QUAD - BY_POOL)
        g_mix, g_out, g_ffn = cols[:, 0:8], cols[:, 8:16], cols[:, 16:24]
        conv_w = cols[:, 24:36].rearrange("p (c w) -> p c w", w=3)

        acc = ctx.enter_context(nc.psum_tensor("acc", [P, 4, 512], f32))
        front = ctx.enter_context(nc.psum_tensor("front", [P, 4, 512], f32))
        work, proj = [front[:, b, :] for b in range(2)], [front[:, 2 + b, :] for b in range(2)]

        def acc_view(k):
            return acc[:, k // 2, (k % 2) * T:(k % 2 + 1) * T]

        def held_view(r, b):
            return acc[:, :, :].rearrange("p a n -> p (a n)")[:, bass.ds(r * T + b * HELD // 2 * T, T)]

        def mixer_hi(c):
            return w_hi[:, c, :] if c < 2 else act_hi[:, c, :]

        def mixer_lo(c):
            return w_lo[:, c, :] if c < 2 else act_lo[:, c, :]

        routed = [bank[:, :] for bank in work + proj]

        x_spilled = sem("x_spilled")
        x_reloaded = sem("x_reloaded")
        again_high = sem("again_high")
        again_low_pool = sem("again_low_pool")
        again_low_dve = sem("again_low_dve")
        turned = sem("turned")
        x_loaded = [sem(f"x_loaded{t}") for t in range(TT)]
        ident_loaded = sem("ident_loaded")
        cols_loaded = sem("cols_loaded")
        consts_loaded = sem("consts_loaded")
        keys_loaded = sem("keys_loaded")
        gain_loaded = sem("gain_loaded")
        out_stored = sem("out_stored")
        raw_loaded = [sem(f"raw_loaded{s}") for s in range(RING)]
        hi_ready = sem("hi_ready")
        lo_by_pool = sem("lo_by_pool")
        lo_by_dve = sem("lo_by_dve")
        block_used = sem("block_used")
        proj_taken = sem("proj_taken")
        conv_taken = sem("conv_taken")
        act_step = sem("act_step")
        dve_step = sem("dve_step")
        pe_step = sem("pe_step")
        dve_ready = sem("dve_ready")
        scores_ready = sem("scores_ready")
        masked_ready = sem("masked_ready")
        exp_ready = sem("exp_ready")
        probs_ready = sem("probs_ready")
        turned_ready = sem("turned_ready")
        turned_taken = sem("turned_taken")
        head_ready = sem("head_ready")
        heads_taken = sem("heads_taken")
        conv_squared = sem("conv_squared")
        eps_ready = sem("eps_ready")
        squares_summed = sem("squares_summed")
        root_ready = sem("root_ready")
        sums_ready = sem("sums_ready")
        scaled_ready = sem("scaled_ready")
        tile_projected = sem("tile_projected")
        act_high = sem("act_high")
        act_split = sem("act_split")
        total_ready = sem("total_ready")
        result_ready = sem("result_ready")
        key_scores = sem("key_scores")
        key_scores_taken = sem("key_scores_taken")
        topk_step = sem("topk_step")
        hot_ready = sem("hot_ready")
        hot_weighted = sem("hot_weighted")
        scales_ready = sem("scales_ready")
        hot_weighted_act = sem("hot_weighted_act")
        router_ready = sem("router_ready")
        router_act = sem("router_act")
        w_ready = sem("w_ready")
        w_hi_ready = sem("w_hi_ready")
        w_lo_ready = sem("w_lo_ready")

        block = ctx.enter_context(nc.Block())

        def wait_low(eng, n):
            if split_by_pool(n):
                eng.wait_ge(lo_by_pool, pool_splits(n))
            else:
                eng.wait_ge(lo_by_dve, dve_splits(n))

        def piece(g, groups):
            q = groups.index(g)
            return slice(q * D // len(groups), (q + 1) * D // len(groups))

        @block.sync
        def _(sp):
            def load(n, s):
                sp.dma_start(raw[:, s, :], stream[bass.ds(n, 1), :, :].rearrange("a p n -> (a p) n")
                             ).then_inc(raw_loaded[s], 16)

            def refill(first, last, waits):
                with sp.Fori(0, (last - first) // RING) as r:
                    for s in range(RING):
                        semaphore, start, step = waits(s)
                        sp.wait_ge(semaphore, r * step + start)
                        load(r * RING + (first + s), s)

            def taking_turns(first):
                def waits(s):
                    n = first - RING + s
                    if s % 2 == 0:
                        return lo_by_pool, pool_splits(n), 2
                    return lo_by_dve, dve_splits(n), 2
                return waits

            for t in range(TT):
                sp.dma_start(x_sb[:, t, :], x[t * P:(t + 1) * P, :]).then_inc(x_loaded[t], 16)
            for s in range(RING):
                load(s, s)
            refill(RING, CONV0 + RING, taking_turns(RING))
            sp.dma_start(keys_sb, keys.rearrange("p (h n) -> p h n", n=NKEYS)).then_inc(keys_loaded, 16)
            refill(CONV0 + RING, WOUT0 + RING, lambda s: (lo_by_pool, pool_splits(CONV0 + s), RING))
            refill(WOUT0 + RING, POOL0 + RING, taking_turns(WOUT0 + RING))
            refill(POOL0 + RING, HELD0, lambda s: (lo_by_pool, pool_splits(POOL0 + s), RING))
            for s in range(2):
                wait_low(sp, HELD0 - RING + s)
                load(HELD0 + s, s)
            for n in range(HELD0 + 2, PAIR0 + 2):
                wait_low(sp, n - 2)
                load(n, n % 2)
            sp.wait_ge(router_ready, GROUPS)
            for s in (2, 3):
                load(PAIR0 + s, s)
            refill(PAIR0 + RING, MIXED_LO + RING, taking_turns(PAIR0 + RING))
            rest = BLOCKS - 2 * RING

            def by_dve(first):
                return lambda s: (lo_by_dve, dve_splits(first - RING + s), RING)
            refill(MIXED_LO + RING, rest, by_dve(MIXED_LO + RING))
            sp.wait_ge(w_lo_ready, 28)
            sp.dma_start(final_gain, final_g.partition_broadcast(P)).then_inc(gain_loaded, 16)
            sp.dma_start(x_again, x_mixed_dram.rearrange("(t p) n -> p t n", p=P)).then_inc(x_reloaded, 16)
            refill(rest, BLOCKS, by_dve(rest))
            stored = 0
            for t in range(TT):
                for first, last in OUT_PIECES[t]:
                    stored += 1
                    sp.wait_ge(result_ready, stored)
                    sp.dma_start(out[t * P:(t + 1) * P, first * 512:last * 512],
                                 result[:, t, first * 512:last * 512]).then_inc(out_stored, 16)
            sp.wait_ge(out_stored, 16 * stored)

        @block.gpsimd
        def _(pool):
            def split(n, s):
                pool.wait_ge(hi_ready, n + 1)
                pool.tensor_tensor(lo[:, s, :], raw[:, s, :], hi[:, s, :].bitcast(f32),
                                   ALU.subtract).then_inc(lo_by_pool, 1)

            def every_other(first, last):
                with pool.Fori(0, (last - first) // RING) as r:
                    for s in (0, 2):
                        split(r * RING + (first + s), s)

            def every(first, last):
                with pool.Fori(0, (last - first) // RING) as r:
                    for s in range(RING):
                        split(r * RING + (first + s), s)

            every_other(QK0, CONV0)
            every(CONV0, WOUT0)
            every_other(WOUT0, POOL0)
            every(POOL0, HELD0)
            split(HELD0, 0)
            pool.wait_ge(act_step, ACT_PICKED)
            with pool.Fori(0, HELD // RING) as r:
                for b in range(RING):
                    for g in range(SPAN):
                        at = RING * SPAN * r + (b * SPAN + g)
                        pool.wait_ge(hot_ready, at + 1)
                        weight = picked_T[:, 1, bass.ds(at * QUAD, BY_POOL)]
                        pool.tensor_tensor(hot_w[:, g % RING, 0:BY_POOL, :],
                                           hot_i[:, g % RING, :, 0:BY_POOL].rearrange("p n u -> p u n"),
                                           weight.unsqueeze(2).to_broadcast([P, BY_POOL, NKEYS]),
                                           ALU.mult).then_inc(hot_weighted, 1)
                        if g in LOW_AT:
                            if g == LOW_AT[0]:
                                pool.wait_ge(hi_ready, r * RING + (HELD0 + b + 2))
                            s, part = (b + 1) % 2, piece(g, LOW_AT)
                            done = pool.tensor_tensor(lo[:, s, part], raw[:, s, part], hi[:, s, part].bitcast(f32),
                                                      ALU.subtract)
                            if g == LOW_AT[-1]:
                                done.then_inc(lo_by_pool, 1)
            split(PAIR0 + 2, 2)
            every_other(PAIR0 + RING, MIXED_LO)
            pool.wait_ge(again_high, 1)
            pool.tensor_tensor(again_lo[:, 0, :], x_again[:, 0, :], again_hi[:, 0, :].bitcast(f32),
                               ALU.subtract).then_inc(again_low_pool, 1)

        @block.scalar
        def _(act):
            def high(n, s, loaded=None):
                act.wait_ge(raw_loaded[s], 16 * raw_use(n) if loaded is None else loaded)
                act.activation(hi[:, s, :], raw[:, s, :], ACT.Copy).then_inc(hi_ready, 1)

            def highs(first, r, s):
                high(None, s, r * 16 + 16 * raw_use(first + s))

            def norm(which, source, scratch, waits):
                for t in range(TT):
                    act.wait_ge(*waits[t])
                    act.activation(scratch(t), source(t), ACT.Square,
                                   accum_out=sumsq[:, which, t:t + 1]).then_inc(squares_summed, 1)
                    act.wait_ge(squares_summed, TT * which + t + 1)
                    act.activation(root[:, t:t + 1], sumsq[:, which, t:t + 1], ACT.Sqrt, bias=eps,
                                   scale=1.0 / D).then_inc(root_ready, 1)

            def transposed_high(gains, first):
                for k in range(KC):
                    act.wait_ge(turned, first + k // 2 + 1)
                    done = act.activation(act_hi[:, k, :], acc_view(k), ACT.Copy, scale=gains[:, k:k + 1])
                    if k % 2:
                        done.then_inc(act_high, 1)

            act.preload_act_table(ACT.Sqrt)
            act.dma_start(ident[:, :], consts[:, 0:128]).then_inc(ident_loaded, 16)
            act.dma_start(cols[:, :], columns).then_inc(cols_loaded, 16)
            act.dma_start(iota[:, :], consts[:, 128:256]).then_inc(consts_loaded, 16)
            act.dma_start(consts_front, consts[:, 256:768]).then_inc(consts_loaded, 16)
            act.wait_ge(eps_ready, 1)
            norm(NORM_X, lambda t: x_sb[:, t, :], lambda t: square_x[:, t, :], [(x_loaded[t], 16) for t in range(TT)])
            high(0, 0)
            high(1, 1)
            act.wait_ge(cols_loaded, 16)
            transposed_high(g_mix, 0)
            high(2, 2)
            high(3, 3)
            with act.Fori(0, (V0 - QK0) // RING) as r:
                for s in range(RING):
                    act.wait_ge(block_used, r * RING + (s + 1))
                    act.activation(qk_T[:, bass.ds(r * RING + s, 1), :], proj[s % 2][:, 0:T].unsqueeze(1),
                                   ACT.Copy).then_inc(proj_taken, 1)
                    highs(RING, r, s)
            for n in range(V0, CONV0):
                act.wait_ge(block_used, n + 1)
                if n == CONV0 - 1:
                    act.activation(v_sb, acc[:, 0:2, :], ACT.Copy).then_inc(act_step, 1)
                high(n + RING, n % RING)

            def mixer_high(c):
                if c < 4:
                    act.wait_ge(conv_taken, 2 * c + 2)
                act.activation(mixer_hi(c), mixer_T[:, c, :], ACT.Copy, scale=g_out[:, c:c + 1]).then_inc(act_high, 1)

            for st in range(WOUT0 - CONV0):
                n, c = CONV0 + st, st // 3
                act.wait_ge(block_used, n + 1)
                if st % 3 == 0:
                    if c >= 2:
                        act.wait_ge(conv_taken, 2 * (c - 2) + 1)
                    act.activation(c_gate[:, c % 2, :], proj[n % 2][:, 0:T], ACT.Copy).then_inc(proj_taken, 1)
                if 2 <= st < HEADS + 2:
                    h = st - 2
                    act.wait_ge(turned_ready, h + 1)
                    if h >= 2:
                        act.wait_ge(head_ready, h - 1)
                    act.activation(probs_T[:, h % 2, :], acc[:, 2 + h % 2, 0:384], ACT.Copy
                                   ).then_inc(turned_taken, 1)
                if st < HEADS:
                    b = st % 2
                    act.wait_ge(masked_ready, st + 1)
                    if st >= 2:
                        act.wait_ge(turned_ready, st - 1)
                    act.activation(probs[:, b, 0:P], masked[:, b, 0:P], ACT.Exp,
                                   bias=neg_max[:, b, 0:1], accum_out=prob_sum[:, b, 0:1])
                    act.activation(probs[:, b, P:384], masked[:, b, P:384], ACT.Exp,
                                   bias=neg_max[:, b, 1:2], accum_out=prob_sum[:, b, 1:2]
                                   ).then_inc(exp_ready, 1)
                if 3 <= st < HEADS + 3 and st % 2 == 0:
                    h = st - 3
                    act.wait_ge(head_ready, h + 1)
                    act.activation(mixer_T[:, 4 + h // 2, :], acc[:, (h // 2) % 2, 0:T], ACT.Copy)
                    act.activation(mixer_sq[:, 4 + h // 2, :], acc[:, (h // 2) % 2, 0:T], ACT.Square
                                   ).then_inc(heads_taken, 1)
                high(n + RING, n % RING)
                if st == HEADS:
                    act.preload_act_table(ACT.Sqrt)
                if st >= WOUT0 - CONV0 - 2:
                    mixer_high(st - (WOUT0 - CONV0 - 2))
            for c in range(2, KC):
                mixer_high(c)
            for c in range(4):
                act.activation(mixer_sq[:, c, :], mixer_T[:, c, :], ACT.Square).then_inc(conv_squared, 1)
            for k in range(KC - 1):
                act.wait_ge(block_used, WOUT0 + k + 1)
                high(WOUT0 + RING + k, k % RING)
                if k == 2:
                    act.wait_ge(pe_step, PE_NORMS)
                    act.activation(root_mixer, work[0][:, 0:2 * TT], ACT.Sqrt, bias=eps,
                                   scale=1.0 / 512).then_inc(act_step, 1)
            norm(NORM_X_MIXED, lambda t: x_mixed[:, t, :], lambda t: square_x[:, t, :],
                 [(dve_ready, X_MIXED + t) for t in range(TT)])
            act.dma_start(x_mixed_dram.rearrange("(t p) n -> p t n", p=P), x_mixed).then_inc(x_spilled, 16)
            transposed_high(g_ffn, KC // 2)
            act.wait_ge(block_used, WQ0)
            high(WQ0 + RING - 1, RING - 1)

            def key_scores_out(q):
                for t in range(TT):
                    act.wait_ge(key_scores, TT * q + t + 1)
                    act.activation(scores[:, t, 4 * q:4 * q + 4, :],
                                   work[t][:, :].rearrange("p (h n) -> p h n", n=NKEYS),
                                   ACT.Copy).then_inc(key_scores_taken, 1)

            for k in range(DOWN0 - WQ0):
                act.wait_ge(block_used, WQ0 + k + 1)
                act.activation(query_T[:, k, :], proj[k % 2][:, 0:T], ACT.Copy).then_inc(proj_taken, 1)
                high(WQ0 + k + RING, k % RING)
                if k >= 6 and k % 4 == 2:
                    key_scores_out((k - 6) // 4)
            key_scores_out(3)
            act.preload_act_table(ACT.Gelu)
            with act.Fori(0, EARLY // RING - 1) as r:
                for s in range(RING):
                    act.wait_ge(block_used, r * RING + (DOWN0 + s + 1))
                    act.activation(experts[:, bass.ds(r * RING + s, 1), :], proj[s % 2][:, 0:T].unsqueeze(1),
                                   ACT.Gelu).then_inc(proj_taken, 1)
                    highs(DOWN0 + RING, r, s)
            for s in range(RING):
                i = EARLY - RING + s
                act.wait_ge(block_used, DOWN0 + i + 1)
                act.activation(experts[:, i, :], proj[s % 2][:, 0:T], ACT.Gelu).then_inc(proj_taken, 1)
                if s == 0:
                    high(HELD0, 0)
                    act.wait_ge(dve_ready, PICKED_SCORES)
                    act.activation(picked[:, 2], picked[:, 2], ACT.Exp).then_inc(act_step, 1)
                    act.preload_act_table(ACT.Gelu)
                if s == RING - 2:
                    act.wait_ge(pe_step, PE_PICKED)
                    act.activation(picked_i[:, :], work[0][:, 0:T], ACT.Copy)
                    act.activation(picked_T[:, 0, :], work[0][:, T:2 * T], ACT.Copy)
                    act.activation(picked_T[:, 1, :], work[1][:, 0:T], ACT.Copy).then_inc(act_step, 1)
            act.wait_ge(x_spilled, 16)

            def weight(g, s, scale):
                act.wait_ge(hot_ready, g + 1)
                for u in range(BY_POOL, QUAD):
                    done = act.activation(hot_w[:, s, u, :], hot_i[:, s, :, u], ACT.Copy,
                                          scale=scale[:, u - BY_POOL:u - BY_POOL + 1])
                done.then_inc(hot_weighted_act, 1)

            def take_scales(r, b, count):
                first = r * (2 * SPAN * QUAD) + (b * SPAN + LOOK) * QUAD
                ahead = picked_T[:, 1, bass.ds(first, count * QUAD)].rearrange("p (g u) -> p g u", u=QUAD)
                act.activation(scales[:, b % 2, 0:count], ahead[:, :, BY_POOL:QUAD], ACT.Copy
                               ).then_inc(scales_ready, 1)

            def held_row(r, b, count=SPAN, next_count=SPAN):
                act.wait_ge(scales_ready, r * 2 + (b + 1))
                for g in range(SPAN):
                    at = r * (2 * SPAN) + (b * SPAN + g)
                    if g in HIGH_AT:
                        slot, part = (b + 1) % 2, piece(g, HIGH_AT)
                        if g == HIGH_AT[0]:
                            act.wait_ge(raw_loaded[slot], r * 16 + 16 * raw_use(HELD0 + b + 1))
                        done = act.activation(hi[:, slot, part], raw[:, slot, part], ACT.Copy)
                        if g == HIGH_AT[-1]:
                            done.then_inc(hi_ready, 1)
                    if g == SPAN // 2 and next_count:
                        take_scales(r, b + 1, next_count)
                    if g < count:
                        weight(at + LOOK, (g + LOOK) % RING, scales[:, b, g, :])
                    act.wait_ge(router_ready, at + 1)
                    act.activation(experts[:, EARLY:NKEYS, bass.ds(at * QUAD, QUAD)]
                                   .rearrange("p i u -> p u i"),
                                   routed[g % RING].rearrange("p (u i) -> p u i", i=NKEYS)[:, :, EARLY:NKEYS],
                                   ACT.Copy).then_inc(router_act, 1)
                act.wait_ge(block_used, r * 2 + (HELD0 + b + 1))
                act.activation(held_view(r, b), held_view(r, b), ACT.Gelu).then_inc(proj_taken, 1)

            for g in range(LOOK):
                weight(g, g, picked_T[:, 1, g * QUAD + BY_POOL:g * QUAD + QUAD])
            take_scales(0, 0, SPAN)
            with act.Fori(0, HELD // 2 - 1) as r:
                for b in range(2):
                    held_row(r, b)
            held_row(HELD // 2 - 1, 0, SPAN, SPAN - LOOK)
            held_row(HELD // 2 - 1, 1, SPAN - LOOK, 0)
            high(PAIR0 + 1, 1)

            def weight_high(m, b, ready):
                act.wait_ge(w_ready, ready)
                act.activation(w_hi[:, b, :].unsqueeze(1), experts[:, m, :], ACT.Copy).then_inc(w_hi_ready, 1)

            for b in range(2):
                weight_high(slice(b, b + 1), b, b + 1)
            for s in (2, 3):
                high(PAIR0 + s, s)
            with act.Fori(0, PAIRS // 2) as r:
                for b in range(2):
                    act.wait_ge(block_used, r * 4 + (PAIR0 + 2 * b + 1))
                    act.wait_ge(w_ready, r * 2 + (AHEAD + b - 1))
                    act.activation(gelu_ring[:, b, :], proj[b][:, 0:T], ACT.Gelu).then_inc(proj_taken, 1)
                    highs(PAIR0 + RING, r, 2 * b)
                    act.wait_ge(block_used, r * 4 + (PAIR0 + 2 * b + 2))
                    weight_high(bass.ds(r * 2 + (b + 2), 1), b, r * 2 + (b + 3))
                    highs(PAIR0 + RING, r, 2 * b + 1)
            with act.Fori(0, AHEAD // RING - 1) as r:
                for s in range(RING):
                    act.wait_ge(block_used, r * RING + (UP0 + s + 1))
                    weight_high(bass.ds(r * RING + (PAIRS + s + 2), 1), s % 2, r * RING + (PAIRS + s + 3))
                    highs(UP0 + RING, r, s)
            act.wait_ge(x_reloaded, 16)
            act.activation(ident_r[:, :], ident[:, :], ACT.Copy)
            for t in range(TT):
                act.activation(again_hi[:, t, :], x_again[:, t, :], ACT.Copy).then_inc(again_high, 1)
            for s in range(2):
                m = NKEYS - 2 + s
                act.wait_ge(block_used, BLOCKS - RING + s + 1)
                weight_high(slice(m, m + 1), s, m + 1)
            act.preload_act_table(ACT.Sqrt)
            norm(NORM_FINAL, lambda t: acc[:, 2 * t:2 * t + 2, :].rearrange("p a n -> p (a n)"),
                 lambda t: final_sq[t], [(total_ready, t + 1) for t in range(TT)])

        @block.vector
        def _(dve):
            chain = [0]

            def link(done):
                chain[0] += 1
                done.then_inc(dve_step, 1)
                dve.wait_ge(dve_step, chain[0])

            def low(n, s):
                dve.wait_ge(hi_ready, n + 1)
                dve.tensor_tensor(lo[:, s, :], raw[:, s, :], hi[:, s, :].bitcast(f32),
                                  ALU.subtract).then_inc(lo_by_dve, 1)

            def scaled(which, source):
                for t in range(TT):
                    dve.wait_ge(root_ready, TT * which + t + 1)
                    link(dve.reciprocal(rstd[:, t:t + 1], root[:, t:t + 1]))
                    dve.tensor_scalar(x_scaled[:, t, :], source[:, t, :], rstd[:, t:t + 1], None,
                                      ALU.mult).then_inc(scaled_ready, 1)

            def transposed_low(gains, first):
                for k in range(KC):
                    dve.wait_ge(act_high, first + k // 2 + 1)
                    done = dve.scalar_tensor_tensor(act_lo[:, k, :], acc_view(k), gains[:, k:k + 1],
                                                    act_hi[:, k, :].bitcast(f32), ALU.mult, ALU.subtract)
                    if k % 2:
                        done.then_inc(act_split, 1)

            dve.memset(eps, EPS).then_inc(eps_ready, 1)
            scaled(NORM_X, x_sb)
            dve.memset(padded[:, :, 0:2], 0.0)
            low(1, 1)
            transposed_low(g_mix, SPLIT_X)
            low(3, 3)
            for n in range(5, CONV0, 2):
                low(n, n % RING)

            def mixer_low_part(c):
                dve.wait_ge(act_high, SPLIT_MIXER + c + 1)
                dve.scalar_tensor_tensor(mixer_lo(c), mixer_T[:, c, :], g_out[:, c:c + 1],
                                         mixer_hi(c).bitcast(f32), ALU.mult, ALU.subtract).then_inc(act_split, 1)

            dve.wait_ge(consts_loaded, 32)
            for st in range(WOUT0 - CONV0 + 1):
                n, c = CONV0 + st, st // 3
                if 1 <= st <= HEADS:
                    h = st - 1
                    b = h % 2
                    dve.wait_ge(exp_ready, h + 1)
                    link(dve.reciprocal(prob_inv[:, b, :], prob_sum[:, b, :]))
                    dve.tensor_scalar(probs[:, b, 0:P], probs[:, b, 0:P], prob_inv[:, b, 0:1], None, ALU.mult)
                    dve.tensor_scalar(probs[:, b, P:384], probs[:, b, P:384], prob_inv[:, b, 1:2], None,
                                      ALU.mult).then_inc(probs_ready, 1)
                if st == WOUT0 - CONV0:
                    break
                if st % 3 == 1:
                    dve.wait_ge(proj_taken, 8 + c + 1)
                    dve.wait_ge(block_used, n + 1)
                    b = c % 2
                    done = dve.tensor_tensor(padded[:, b, 2:T + 2], proj[n % 2][:, 0:T], c_gate[:, b, :], ALU.mult)
                    done.then_inc(conv_taken, 1)
                    dve.wait_ge(conv_taken, 2 * c + 1)
                    link(dve.tensor_scalar(taps[:, b, 0, :], padded[:, b, 2:T + 2], conv_w[:, c, 2:3], None, ALU.mult))
                    link(dve.scalar_tensor_tensor(taps[:, b, 1, :], padded[:, b, 1:T + 1], conv_w[:, c, 1:2],
                                                  taps[:, b, 0, :], ALU.mult, ALU.add))
                    link(dve.scalar_tensor_tensor(taps[:, b, 2, :], padded[:, b, 0:T], conv_w[:, c, 0:1],
                                                  taps[:, b, 1, :], ALU.mult, ALU.add))
                if st % 3 == 2:
                    dve.wait_ge(block_used, n + 1)
                    dve.tensor_tensor(mixer_T[:, c, :], proj[n % 2][:, 0:T], taps[:, c % 2, 2, :],
                                      ALU.mult).then_inc(conv_taken, 1)
                if st < HEADS:
                    b = st % 2
                    dve.wait_ge(scores_ready, st + 1)
                    if st >= 2:
                        dve.wait_ge(exp_ready, st - 1)
                    link(dve.scalar_tensor_tensor(masked[:, b, :], work[b][:, 0:384], float(HD) ** -0.5,
                                                  mask, ALU.mult, ALU.add))
                    dve.reduce_max(neg_max[:, b, 0:1], masked[:, b, 0:P], AX.X, negate=True)
                    dve.reduce_max(neg_max[:, b, 1:2], masked[:, b, P:384], AX.X, negate=True
                                   ).then_inc(masked_ready, 1)
                if n + RING >= WOUT0 and n % 2:
                    low(n + RING, n % RING)
                if st >= WOUT0 - CONV0 - 2:
                    mixer_low_part(st - (WOUT0 - CONV0 - 2))
            for c in range(2, KC):
                mixer_low_part(c)
            dve.wait_ge(conv_squared, 4)
            for half in range(2):
                done = dve.reduce_sum(square_sums[:, half, :],
                                      mixer_sq[:, 4 * half:4 * half + 4, :].rearrange("p c t -> p t c"), AX.X)
            done.then_inc(sums_ready, 1)
            low(WOUT0 + RING + 1, 1)
            dve.wait_ge(act_step, ACT_ROOT_MIXER)
            link(dve.reciprocal(rstd_mixer, root_mixer))
            low(WOUT0 + RING + 3, 3)

            def normed(t, half, banks, added):
                return dve.scalar_tensor_tensor(
                    x_mixed[:, t, :].rearrange("p (a n) -> p a n", a=2), banks[:, 2 * t:2 * t + 2, :],
                    rstd_mixer[:, half * TT + t:half * TT + t + 1],
                    added[:, t, :].rearrange("p (a n) -> p a n", a=2), ALU.mult, ALU.add)

            dve.wait_ge(block_used, WOUT0 + 4)
            for t in range(TT):
                link(normed(t, 0, acc, x_sb))
            low(WQ0 + 1, 1)
            for t in range(TT):
                if t == TT - 1:
                    dve.wait_ge(block_used, WQ0)
                else:
                    dve.wait_ge(tile_projected, t + 1)
                normed(t, 1, front, x_mixed).then_inc(dve_ready, 1)
            scaled(NORM_X_MIXED, x_mixed)
            transposed_low(g_ffn, SPLIT_X_MIXED)
            low(WQ0 + RING - 1, RING - 1)

            taken = [0]

            def step(done):
                taken[0] += 1
                done.then_inc(topk_step, 1)
                return taken[0]

            def top16(values, left, best, at, rows):
                first = [step(dve.max(best[:, h, 0:8], values[:, h, :])) for h in range(rows)]
                for h in range(rows):
                    dve.wait_ge(topk_step, first[h])
                    step(dve.max_index(at[:, h, 0:8], best[:, h, 0:8], values[:, h, :]))
                rest = []
                for h in range(rows):
                    rest.append(step(dve.match_replace(left[:, h, :], best[:, h, 0:8], values[:, h, :], LOWEST)))
                second = []
                for h in range(rows):
                    dve.wait_ge(topk_step, rest[h])
                    second.append(step(dve.max(best[:, h, 8:16], left[:, h, :])))
                for h in range(rows):
                    dve.wait_ge(topk_step, second[h])
                    last = step(dve.max_index(at[:, h, 8:16], best[:, h, 8:16], left[:, h, :]))
                dve.wait_ge(topk_step, last)

            for q in range(4):
                for t in range(TT):
                    rows = slice(4 * q, 4 * q + 4)
                    dve.wait_ge(key_scores_taken, TT * q + t + 1)
                    top16(scores[:, t, rows, :], scores_left, top1[:, t, rows, :], top1_at[:, t, rows, :], 4)
            for t in range(TT):
                link(dve.tensor_copy(first_index, top1_at[:, t]))
                halves = top1[:, t].rearrange("p (h a) k -> p h a k", a=2)
                link(dve.tensor_tensor(
                    pairs.rearrange("p h (a b) -> p h a b", b=TOPK),
                    halves[:, :, 0, :].unsqueeze(3).to_broadcast([P, PH, TOPK, TOPK]),
                    halves[:, :, 1, :].unsqueeze(2).to_broadcast([P, PH, TOPK, TOPK]), ALU.add))
                best = picked[:, 2, t, :].rearrange("p (h k) -> p h k", k=TOPK)
                top16(pairs, pairs_left, best, pos.rearrange("p (h k) -> p h k", k=TOPK), PH)
                dve.tensor_scalar(pos_ab[:, 0, :], pos, 4, None, ALU.logical_shift_right)
                link(dve.tensor_scalar(pos_ab[:, 1, :], pos, 15, None, ALU.bitwise_and))
                link(dve.tensor_copy(ranks, pos_ab))
                for a in range(2):
                    link(dve.tensor_tensor(lookup,
                                           iota[:, 0:TOPK].unsqueeze(1).to_broadcast([P, PH * TOPK, TOPK]),
                                           ranks[:, a, :].unsqueeze(2).to_broadcast([P, PH * TOPK, TOPK]),
                                           ALU.is_equal))
                    spread = lookup.rearrange("p (h k) a -> p h k a", k=TOPK)
                    number = first_index.rearrange("p (h a) k -> p h a k", a=2)[:, :, a, :]
                    link(dve.tensor_tensor(spread, spread,
                                           number.unsqueeze(2).to_broadcast([P, PH, TOPK, TOPK]), ALU.mult))
                    link(dve.reduce_sum(picked[:, a, t, :], lookup, AX.X))
                peak = stats[:, 40:48]
                link(dve.tensor_copy(peak, best[:, :, 0]))
                link(dve.tensor_tensor(best, best, peak.unsqueeze(2).to_broadcast([P, PH, TOPK]), ALU.subtract))
            dve.memset(gate_sum, 0.0).then_inc(dve_ready, 1)
            dve.wait_ge(dve_ready, PICKED_SCORES)
            dve.wait_ge(act_step, ACT_EXP)
            gates = picked[:, 2].rearrange("p t (h k) -> p (t h) k", k=TOPK)
            link(dve.reduce_sum(gate_sum, gates, AX.X))
            link(dve.reciprocal(gate_sum, gate_sum))
            link(dve.tensor_tensor(gates, gates, gate_sum.unsqueeze(2).to_broadcast([P, TT * PH, TOPK]), ALU.mult))
            assert chain[0] == DVE_PICKED, chain[0]

            def hots(g, s):
                group = bass.ds(g * QUAD, QUAD)
                dve.tensor_tensor(hot_j[s], iota[:, :].unsqueeze(1).to_broadcast([P, QUAD, NKEYS]),
                                  picked_T[:, 0, group].unsqueeze(2).to_broadcast([P, QUAD, NKEYS]), ALU.is_equal)
                dve.tensor_tensor(hot_i[:, s], iota_quad[:, :, :],
                                  picked_i[:, group].unsqueeze(1).to_broadcast([P, NKEYS, QUAD]),
                                  ALU.is_equal).then_inc(hot_ready, 1)

            def rows_in_place(g, s):
                dve.wait_ge(router_act, g + 1)
                rows = experts[:, 0:EARLY, bass.ds(g * QUAD, QUAD)].rearrange("p i u -> p u i")
                return dve.tensor_tensor(rows, routed[s].rearrange("p (u i) -> p u i", i=NKEYS)[:, :, 0:EARLY],
                                         rows, ALU.mult)

            link(dve.tensor_copy(iota_quad[:, :, :], iota[:, :].unsqueeze(2).to_broadcast([P, NKEYS, QUAD])))
            dve.wait_ge(act_step, ACT_PICKED)
            dve.wait_ge(lo_by_pool, pool_splits(HELD0 - 1))
            for s in range(RING):
                hots(s, s)
            with dve.Fori(0, GROUPS // RING - 1) as r:
                for s in range(RING):
                    rows_in_place(r * RING + s, s)
                    hots(r * RING + (RING + s), s)
            for s in range(RING - 1):
                rows_in_place(GROUPS - RING + s, s)
            rows_in_place(GROUPS - 1, RING - 1).then_inc(w_ready, EARLY)

            def weight_low(m, b, ready):
                dve.wait_ge(w_hi_ready, ready)
                dve.tensor_tensor(w_lo[:, b, :].unsqueeze(1), experts[:, m, :],
                                  w_hi[:, b, :].bitcast(f32).unsqueeze(1), ALU.subtract).then_inc(w_lo_ready, 1)

            dve.wait_ge(proj_taken, 28 + AHEAD)
            rows = experts[:, EARLY:AHEAD, :].rearrange("p (r b) t -> p b r t", b=2)
            held = acc[:, :, :].rearrange("p a n -> p (a n)").rearrange("p (b r t) -> p b r t", b=2, t=T)
            dve.tensor_tensor(rows, held, rows, ALU.mult).then_inc(w_ready, HELD)
            low(PAIR0 + 1, 1)
            for b in range(2):
                weight_low(slice(b, b + 1), b, b + 1)
            low(PAIR0 + 3, 3)
            with dve.Fori(0, PAIRS // 2) as r:
                for b in range(2):
                    dve.wait_ge(proj_taken, r * 2 + (28 + AHEAD + b + 1))
                    row = experts[:, bass.ds(r * 2 + (AHEAD + b), 1), :]
                    dve.tensor_tensor(row, row, gelu_ring[:, b, :].unsqueeze(1), ALU.mult).then_inc(w_ready, 1)
                    weight_low(bass.ds(r * 2 + (b + 2), 1), b, r * 2 + (b + 3))
                    low(r * RING + (PAIR0 + RING + 2 * b + 1), 2 * b + 1)
            with dve.Fori(0, AHEAD // RING - 1) as r:
                for s in range(RING):
                    weight_low(bass.ds(r * RING + (PAIRS + s + 2), 1), s % 2, r * RING + (PAIRS + s + 3))
                    low(r * RING + (UP0 + RING + s), s)
            dve.wait_ge(again_high, 2)
            dve.tensor_tensor(again_lo[:, 1, :], x_again[:, 1, :], again_hi[:, 1, :].bitcast(f32),
                              ALU.subtract).then_inc(again_low_dve, 1)
            for s in range(2):
                m = NKEYS - 2 + s
                weight_low(slice(m, m + 1), s, m + 1)

            dve.wait_ge(gain_loaded, 16)
            for t in range(TT):
                dve.wait_ge(root_ready, TT * NORM_FINAL + t + 1)
                link(dve.reciprocal(rstd[:, t:t + 1], root[:, t:t + 1]))
                for first, last in OUT_PIECES[t]:
                    dve.scalar_tensor_tensor(
                        result[:, t, first * 512:last * 512],
                        acc[:, 2 * t + first:2 * t + last, :].rearrange("p a n -> p (a n)"), rstd[:, t:t + 1],
                        final_gain[:, first * 512:last * 512], ALU.mult, ALU.mult).then_inc(result_ready, 1)

        @block.tensor
        def _(pe):
            def rows_product(s, target, split=None):
                for k in range(KC):
                    if split is not None and k % 2 == 0:
                        pe.wait_ge(act_split, split + k // 2 + 1)
                    part = slice(k * P, (k + 1) * P)
                    pe.matmul(target, hi[:, s, part], act_hi[:, k, :], start=(k == 0), stop=False)
                    pe.matmul(target, hi[:, s, part], act_lo[:, k, :], start=False, stop=False)
                    done = pe.matmul(target, lo[:, s, part], act_hi[:, k, :], start=False, stop=(k == KC - 1))
                return done

            def token_product(left_hi, left_lo, right, target, width, start, stop, tiles=range(TT)):
                for t in tiles:
                    part = slice(t * P, (t + 1) * P)
                    for left, rights in ((left_hi, (hi, lo)), (left_lo, (hi,))):
                        for r in rights:
                            for half in range(width):
                                done = pe.matmul(target(t, half), left[:, part], right(r, half),
                                                 start=start and left is left_hi and r is hi,
                                                 stop=stop and left is left_lo)
                return done

            def transposes(which):
                for t in range(TT):
                    pe.wait_ge(scaled_ready, TT * which + t + 1)
                    for k in range(KC):
                        done = pe.transpose(acc_view(k)[:, t * P:(t + 1) * P],
                                            x_scaled[:, t, k * P:(k + 1) * P], ident[:, :])
                        if t == TT - 1 and k % 2:
                            done.then_inc(turned, 1)

            pe.wait_ge(ident_loaded, 16)
            transposes(NORM_X)
            for n in range(QK0, V0):
                wait_low(pe, n)
                if n >= 2:
                    pe.wait_ge(proj_taken, n - 1)
                rows_product(n % RING, proj[n % 2][:, 0:T], SPLIT_X if n == 0 else None).then_inc(block_used, 1)
            for n in range(V0, CONV0):
                wait_low(pe, n)
                s = n % RING
                for c in range(2):
                    k = 2 * (n - V0) + c
                    done = token_product(act_hi[:, k, :], act_lo[:, k, :],
                                         lambda r, half: r[:, s, c * 512:(c + 1) * 512],
                                         lambda t, half: acc[:, t, :], 1, k == 0, k == KC - 1)
                done.then_inc(block_used, 1)
            for st in range(WOUT0 - CONV0):
                n, c = CONV0 + st, st // 3
                wait_low(pe, n)
                if st >= 2:
                    before = st - 2
                    if before % 3 == 0:
                        pe.wait_ge(proj_taken, 8 + before // 3 + 1)
                    else:
                        pe.wait_ge(conv_taken, 2 * (before // 3) + before % 3)
                else:
                    pe.wait_ge(proj_taken, 8)
                rows_product(n % RING, proj[n % 2][:, 0:T]).then_inc(block_used, 1)
                if st < HEADS:
                    if st >= 2:
                        pe.wait_ge(masked_ready, st - 1)
                    rows = slice(HD * (st % 2), HD * (st % 2) + HD)
                    q, k = qk_T[rows, st // 2, :], qk_T[rows, 4 + st // 2, :]
                    pe.matmul(work[st % 2][:, 0:P], q[:, 0:P], k[:, 0:P], start=True, stop=True)
                    pe.matmul(work[st % 2][:, P:384], q[:, P:T], k, start=True, stop=True
                              ).then_inc(scores_ready, 1)
                if 2 <= st < HEADS + 2:
                    h = st - 2
                    pe.wait_ge(probs_ready, h + 1)
                    if h >= 2:
                        pe.wait_ge(turned_taken, h - 1)
                    for b in range(3):
                        done = pe.transpose(acc[:, 2 + h % 2, b * P:(b + 1) * P],
                                            probs[:, h % 2, b * P:(b + 1) * P], ident[:, :])
                    done.then_inc(turned_ready, 1)
                if 3 <= st < HEADS + 3:
                    h = st - 3
                    pe.wait_ge(turned_taken, h + 1)
                    if h == 0:
                        pe.wait_ge(act_step, ACT_V)
                    if h >= 4 and h % 2 == 0:
                        pe.wait_ge(heads_taken, h // 2 - 1)
                    rows = slice(HD * (h % 2), HD * (h % 2) + HD)
                    target = acc[rows, (h // 2) % 2, :]
                    vh = v_sb[:, :, h * HD:(h + 1) * HD]
                    pe.matmul(target[:, 0:P], vh[:, 0, :], probs_T[:, h % 2, 0:P], start=True, stop=True)
                    pe.matmul(target[:, P:T], vh[:, 0, :], probs_T[:, h % 2, P:2 * P], start=True, stop=False)
                    pe.matmul(target[:, P:T], vh[:, 1, :], probs_T[:, h % 2, 2 * P:384], start=False,
                              stop=True).then_inc(head_ready, 1)
            def mixer_sums():
                pe.wait_ge(consts_loaded, 32)
                pe.wait_ge(sums_ready, 1)
                for half in range(2):
                    for t in range(TT):
                        at = half * TT + t
                        done = pe.matmul(work[0][:, at:at + 1], square_sums[:, half, t * P:(t + 1) * P],
                                         ones[:, 0:1], start=True, stop=True)
                done.then_inc(pe_step, 1)

            pe.wait_ge(heads_taken, 4)
            for n in range(WOUT0, WQ0):
                wait_low(pe, n)
                s, c = n % RING, n - WOUT0
                pe.wait_ge(act_split, SPLIT_MIXER + c + 1)
                if c == 4:
                    pe.wait_ge(act_step, ACT_ROOT_MIXER)
                banks = front if c >= 4 else acc
                for t in range(TT):
                    done = token_product(mixer_hi(c), mixer_lo(c),
                                         lambda r, half: r[:, s, half * 512:(half + 1) * 512],
                                         lambda t, half: banks[:, 2 * t + half, :], 2, c % 4 == 0, c % 4 == 3, [t])
                    if c == KC - 1 and t < TT - 1:
                        done.then_inc(tile_projected, 1)
                done.then_inc(block_used, 1)
                if c == 2:
                    mixer_sums()
            transposes(NORM_X_MIXED)

            def key_products(q):
                pe.wait_ge(proj_taken, 12 + 4 * q + 4)
                for t in range(TT):
                    if q:
                        pe.wait_ge(key_scores_taken, TT * (q - 1) + t + 1)
                    for h in range(4):
                        row = 4 * q + h
                        done = pe.matmul(work[t][:, h * NKEYS:(h + 1) * NKEYS],
                                         query_T[:, row, t * P:(t + 1) * P], keys_sb[:, row, :],
                                         start=True, stop=True)
                    done.then_inc(key_scores, 1)

            pe.wait_ge(keys_loaded, 16)
            for k in range(DOWN0 - WQ0):
                wait_low(pe, WQ0 + k)
                pe.wait_ge(proj_taken, 12 + k - 1)
                rows_product(k % RING, proj[k % 2][:, 0:T], SPLIT_X_MIXED if k == 0 else None
                             ).then_inc(block_used, 1)
                if k >= 5 and k % 4 == 1:
                    key_products((k - 5) // 4)
            key_products(3)
            with pe.Fori(0, EARLY // RING - 1) as r:
                for s in range(RING):
                    pe.wait_ge(lo_by_pool, r * RING + pool_splits(DOWN0 + s))
                    pe.wait_ge(proj_taken, r * RING + (28 + s - 1))
                    rows_product(s, proj[s % 2][:, 0:T]).then_inc(block_used, 1)
            for s in range(RING):
                if s == RING - 1:
                    pe.wait_ge(dve_step, DVE_PICKED)
                    for c in range(3):
                        for t in range(TT):
                            at = (2 * c + t) % 4
                            done = pe.transpose(work[c // 2][:, at * P:(at + 1) * P], picked[:, c, t, :], ident[:, :])
                    done.then_inc(pe_step, 1)
                pe.wait_ge(lo_by_pool, pool_splits(HELD0 - RING + s))
                pe.wait_ge(proj_taken, 28 + EARLY - RING + s - 1)
                rows_product(s, proj[s % 2][:, 0:T]).then_inc(block_used, 1)

            with pe.Fori(0, HELD // RING) as r:
                for b in range(RING):
                    for g in range(SPAN):
                        if g == 0:
                            pe.wait_ge(lo_by_pool, r * RING + pool_splits(HELD0 + b))
                            pe.wait_ge(proj_taken, r * RING + (28 + EARLY + b - 1))
                        part, row = slice(g * P, (g + 1) * P), held_view(r * 2 + b // 2, b % 2)
                        pe.matmul(row, hi[:, b % 2, part], act_hi[:, g, :], start=(g == 0), stop=False)
                        pe.matmul(row, hi[:, b % 2, part], act_lo[:, g, :], start=False, stop=False)
                        done = pe.matmul(row, lo[:, b % 2, part], act_hi[:, g, :], start=False,
                                         stop=(g == KC - 1))
                        if g == KC - 1:
                            done.then_inc(block_used, 1)
                        s = g % RING
                        pe.wait_ge(hot_weighted, RING * SPAN * r + (b * SPAN + g + 1))
                        pe.wait_ge(hot_weighted_act, RING * SPAN * r + (b * SPAN + g + 1))
                        for u in range(QUAD):
                            done = pe.matmul(routed[s][:, u * NKEYS:(u + 1) * NKEYS],
                                             hot_j[s][:, u, :].bitcast(f32), hot_w[:, s, u, :],
                                             start=True, stop=True)
                        done.then_inc(router_ready, 1)

            def up(s, b, stop=False, tiles=range(TT), start=False):
                return token_product(w_hi[:, b, :], w_lo[:, b, :],
                                     lambda r, half: r[:, s, half * 512:(half + 1) * 512],
                                     lambda t, half: acc[:, 2 * t + half, :], 2, start, stop, tiles)

            pe.wait_ge(w_ready, EARLY)

            def pair(r, b, first=False):
                pe.wait_ge(lo_by_pool, r * 2 + pool_splits(PAIR0 + 2 * b))
                pe.wait_ge(proj_taken, r * 2 + (28 + AHEAD + b - 1))
                rows_product(2 * b, proj[b][:, 0:T]).then_inc(block_used, 1)
                pe.wait_ge(lo_by_dve, r * 2 + dve_splits(PAIR0 + 2 * b + 1))
                pe.wait_ge(w_lo_ready, r * 2 + (b + 1))
                if first:
                    pe.wait_ge(w_ready, AHEAD)
                up(2 * b + 1, b, start=first).then_inc(block_used, 1)

            pair(0, 0, True)
            pair(0, 1)
            with pe.Fori(1, PAIRS // 2) as r:
                for b in range(2):
                    pair(r, b)
            for s in range(RING):
                wait_low(pe, UP0 + s)
                pe.wait_ge(w_lo_ready, PAIRS + s + 1)
                up(s, s % 2).then_inc(block_used, 1)
            with pe.Fori(0, AHEAD // RING - 2) as r:
                for s in range(RING):
                    pe.wait_ge(lo_by_dve, r * RING + dve_splits(MIXED_LO + s))
                    pe.wait_ge(w_lo_ready, r * RING + (PAIRS + RING + s + 1))
                    up(s, s % 2).then_inc(block_used, 1)
            for s in range(2):
                wait_low(pe, BLOCKS - RING + s)
                pe.wait_ge(w_lo_ready, NKEYS - RING + s + 1)
                up(s, s % 2).then_inc(block_used, 1)
            pe.wait_ge(again_low_pool, 1)
            pe.wait_ge(again_low_dve, 1)
            for t in range(TT):
                for part in (again_hi, again_lo):
                    for half in range(2):
                        pe.matmul(acc[:, 2 * t + half, :], ident_r[:, :], part[:, t, half * 512:(half + 1) * 512],
                                  start=False, stop=False)
            for s in (2, 3):
                wait_low(pe, BLOCKS - RING + s)
            pe.wait_ge(w_lo_ready, NKEYS)
            for t in range(TT):
                up(2, 0, False, [t])
                up(3, 1, True, [t]).then_inc(total_ready, 1)


def columns_of(w, first, count):
    part = w[:, first:first + count * P].reshape(KC, P, count, P)
    return part.transpose(2, 1, 0, 3).reshape(count, P, D)


def kernel(x, norm_mix_g, w_in, conv_w, norm_conv_out_g, norm_attn_out_g, w_out, norm_ffn_g, peer_w_query,
           peer_sub_keys1, peer_sub_keys2, peer_down, peer_up, final_norm_g):
    import numpy as np
    import concourse.bacc as bacc
    from concourse.bass_utils import run_bass_kernel_spmd

    w_in, w_out, wq = np.asarray(w_in)[0], np.asarray(w_out)[0], np.asarray(peer_w_query)[0]
    down, up = np.asarray(peer_down)[0], np.asarray(peer_up)[0]
    b_cols, c_cols, h_cols = (columns_of(w_in, 512 * g, 4) for g in range(3))
    down = down.reshape(NKEYS, NKEYS, KC, P).transpose(0, 3, 2, 1).reshape(NKEYS, P, D)
    up = up.reshape(NKEYS, NKEYS, D)
    parts = [
        columns_of(w_in, 1536, 8),
        w_in[:, 2560:3072].reshape(4, 2, P, 512).transpose(0, 2, 1, 3).reshape(4, P, D),
        np.stack([g[c] for c in range(4) for g in (c_cols, h_cols, b_cols)]),
        w_out.reshape(KC, P, D),
        columns_of(wq, 0, 16),
        down[:AHEAD],
        np.stack([down[AHEAD:], up[:PAIRS]], axis=1).reshape(2 * PAIRS, P, D),
        up[PAIRS:],
    ]
    stream = np.concatenate(parts)
    keys = np.stack([np.asarray(peer_sub_keys1)[0], np.asarray(peer_sub_keys2)[0]], axis=1)
    keys = np.ascontiguousarray(keys.transpose(3, 0, 1, 2).reshape(P, 2 * PH * NKEYS))

    def column(g):
        return np.asarray(g).reshape(-1, P).T

    taps = np.asarray(conv_w)[0].reshape(3, 4, P).transpose(2, 1, 0).reshape(P, 12)
    columns = np.ascontiguousarray(np.concatenate(
        [column(norm_mix_g[0]), column(norm_conv_out_g[0]), column(norm_attn_out_g[0]), column(norm_ffn_g[0]), taps],
        axis=1))
    n = np.arange(P)
    future = np.where(n[None, :] > n[:, None], NEG, 0.0)
    consts = np.concatenate([np.eye(P), np.tile(n, (P, 1)), future, np.zeros((P, P)), future, np.ones((P, P))],
                            axis=1).astype(np.float32)
    arrays = {
        "x": np.ascontiguousarray(np.asarray(x)[0]), "stream": stream, "keys": keys, "columns": columns,
        "consts": consts, "final_g": np.asarray(final_norm_g),
    }
    nc = bacc.Bacc("TRN2", target_bir_lowering=False, num_devices=1)
    args = [nc.dram_tensor(f"in_{k}", a.shape, mybir.dt.from_np(a.dtype), kind="ExternalInput").ap()
            for k, a in arrays.items()]
    args.append(nc.dram_tensor("x_mixed_dram", (T, D), mybir.dt.float32, kind="Internal").ap())
    args.append(nc.dram_tensor("out_x", (T, D), mybir.dt.float32, kind="ExternalOutput").ap())
    block_kernel(nc, *args)
    r = run_bass_kernel_spmd(nc, [{f"in_{k}": a for k, a in arrays.items()}], core_ids=[0])
    return r.results[0]["out_x"].reshape(1, T, D)
```
